# Optimizing a Trainium2 kernel written in Bass

```python
import math
import jax, jax.numpy as jnp
from jax import lax
import numpy as np

D_MODEL = 1024
BATCH = 1
SEQ = 256
DEPTH = 1

MIX_WIDTH = D_MODEL
S5_WIDTH = D_MODEL // 4
S5_GROUP_DIM = 16
S5_GROUPS = S5_WIDTH // S5_GROUP_DIM
S5_STATE = 64
SSD_INNER = MIX_WIDTH - S5_WIDTH
SSD_HEAD_DIM = 64
SSD_HEADS = SSD_INNER // SSD_HEAD_DIM
SSD_GROUPS = 4
SSD_HPG = SSD_HEADS // SSD_GROUPS
SSD_STATE = 128
SSD_CONV = 4
SSD_CHUNK = 128
SSD_CONV_DIM = SSD_INNER + 2 * SSD_GROUPS * SSD_STATE
IN_COLS = S5_WIDTH + SSD_INNER + SSD_CONV_DIM + SSD_HEADS
MEM_LEN = 256
XA_HEADS = 4
XA_HEAD_DIM = D_MODEL // XA_HEADS
D_FF = 256 * ((8 * D_MODEL // 3 + 255) // 256)
FFN_CONV = 3
NORM_EPS = 1e-6


def rmsnorm(x, w):
    xf = x.astype(jnp.float32)
    xf = xf * lax.rsqrt(jnp.mean(xf * xf, axis=-1, keepdims=True) + NORM_EPS)
    return (xf * w.astype(jnp.float32)).astype(x.dtype)

def causal_dwconv(x, w, b):
    k = w.shape[0]
    l = x.shape[1]
    xp = jnp.pad(x, ((0, 0), (k - 1, 0), (0, 0)))
    y = xp[:, 0:l] * w[0]
    for i in range(1, k):
        y = y + xp[:, i:i + l] * w[i]
    return y + b

def s5_mixer(u, lam_re, lam_im, log_dt, b_re, b_im, c_re, c_im, d_skip, w_glu):
    bsz, l, _ = u.shape
    f32 = jnp.float32
    uf = u.reshape(bsz, l, S5_GROUPS, S5_GROUP_DIM).astype(f32)
    lr = jnp.minimum(lam_re.astype(f32), -1e-4)
    li = lam_im.astype(f32)
    dt = jnp.exp(log_dt.astype(f32))[:, None]
    mag = jnp.exp(lr * dt)
    ab_re = mag * jnp.cos(li * dt)
    ab_im = mag * jnp.sin(li * dt)
    den = lr * lr + li * li
    f_re = ((ab_re - 1.0) * lr + ab_im * li) / den
    f_im = (ab_im * lr - (ab_re - 1.0) * li) / den
    br = b_re.astype(f32)
    bi = b_im.astype(f32)
    bb_re = f_re[..., None] * br - f_im[..., None] * bi
    bb_im = f_re[..., None] * bi + f_im[..., None] * br
    bu_re = jnp.einsum('blgc,gpc->blgp', uf, bb_re)
    bu_im = jnp.einsum('blgc,gpc->blgp', uf, bb_im)
    a_re = jnp.broadcast_to(ab_re, bu_re.shape)
    a_im = jnp.broadcast_to(ab_im, bu_im.shape)

    def combine(e1, e2):
        a1r, a1i, b1r, b1i = e1
        a2r, a2i, b2r, b2i = e2
        return (a2r * a1r - a2i * a1i,
                a2r * a1i + a2i * a1r,
                a2r * b1r - a2i * b1i + b2r,
                a2r * b1i + a2i * b1r + b2i)

    _, _, h_re, h_im = lax.associative_scan(combine, (a_re, a_im, bu_re, bu_im), axis=1)
    y = (jnp.einsum('blgp,gcp->blgc', h_re, c_re.astype(f32))
         - jnp.einsum('blgp,gcp->blgc', h_im, c_im.astype(f32)))
    y = y + uf * d_skip.astype(f32).reshape(S5_GROUPS, S5_GROUP_DIM)
    y = jax.nn.gelu(y.reshape(bsz, l, S5_WIDTH))
    y = y * jax.nn.sigmoid(y @ w_glu.astype(f32))
    return y.astype(u.dtype)

def ssd_mixer(z, xbc, dt_raw, conv_w, conv_b, dt_bias, a_log, d_skip, norm_w):
    bsz, l, _ = xbc.shape
    f32 = jnp.float32
    nc = l // SSD_CHUNK
    xbc = jax.nn.silu(causal_dwconv(xbc, conv_w, conv_b))
    xs = xbc[..., :SSD_INNER]
    bmat = xbc[..., SSD_INNER:SSD_INNER + SSD_GROUPS * SSD_STATE]
    cmat = xbc[..., SSD_INNER + SSD_GROUPS * SSD_STATE:]
    x = xs.reshape(bsz, nc, SSD_CHUNK, SSD_GROUPS, SSD_HPG, SSD_HEAD_DIM)
    bm = bmat.reshape(bsz, nc, SSD_CHUNK, SSD_GROUPS, SSD_STATE)
    cm = cmat.reshape(bsz, nc, SSD_CHUNK, SSD_GROUPS, SSD_STATE)
    dt = jax.nn.softplus(dt_raw.astype(f32) + dt_bias.astype(f32))
    a = -jnp.exp(a_log.astype(f32))
    dt_c = dt.reshape(bsz, nc, SSD_CHUNK, SSD_GROUPS, SSD_HPG)
    da = jnp.moveaxis(dt_c * a.reshape(SSD_GROUPS, SSD_HPG), 2, -1)
    a_cs = jnp.cumsum(da, axis=-1)
    xdt = x.astype(f32) * dt_c[..., None]
    seg = a_cs[..., :, None] - a_cs[..., None, :]
    causal = jnp.tril(jnp.ones((SSD_CHUNK, SSD_CHUNK), dtype=bool))
    lmat = jnp.exp(jnp.where(causal, seg, -jnp.inf))
    cb = jnp.einsum('bclgn,bcsgn->bcgls', cm.astype(f32), bm.astype(f32))
    y_diag = jnp.einsum('bcgls,bcghls,bcsghp->bclghp', cb, lmat, xdt)
    decay_states = jnp.exp(a_cs[..., -1:] - a_cs)
    states = jnp.einsum('bclgn,bcghl,bclghp->bcghpn', bm.astype(f32), decay_states, xdt)
    chunk_decay = jnp.exp(a_cs[..., -1])

    def step(carry, inp):
        st, dec = inp
        return carry * dec[..., None, None] + st, carry

    init = jnp.zeros((bsz, SSD_GROUPS, SSD_HPG, SSD_HEAD_DIM, SSD_STATE), f32)
    _, prev = lax.scan(step, init, (jnp.moveaxis(states, 1, 0), jnp.moveaxis(chunk_decay, 1, 0)))
    prev = jnp.moveaxis(prev, 0, 1)
    y_off = jnp.einsum('bclgn,bcghpn,bcghl->bclghp', cm.astype(f32), prev, jnp.exp(a_cs))
    y = y_diag + y_off + x.astype(f32) * d_skip.astype(f32).reshape(SSD_GROUPS, SSD_HPG)[:, :, None]
    y = y.reshape(bsz, l, SSD_INNER).astype(z.dtype)
    return rmsnorm(y * jax.nn.silu(z), norm_w)

def cross_attention(h, mem_n, wq, wk, wv, wo):
    bsz, l, _ = h.shape
    m = mem_n.shape[1]
    q = (h @ wq).reshape(bsz, l, XA_HEADS, XA_HEAD_DIM)
    k = (mem_n @ wk).reshape(bsz, m, XA_HEADS, XA_HEAD_DIM)
    v = (mem_n @ wv).reshape(bsz, m, XA_HEADS, XA_HEAD_DIM)
    s = jnp.einsum('blhd,bmhd->bhlm', q, k).astype(jnp.float32) * (XA_HEAD_DIM ** -0.5)
    p = jax.nn.softmax(s, axis=-1).astype(v.dtype)
    o = jnp.einsum('bhlm,bmhd->blhd', p, v).reshape(bsz, l, D_MODEL)
    return o @ wo

def conv_ffn(h, w_up, conv_w, conv_b, w_down):
    gv = h @ w_up
    g = causal_dwconv(gv[..., :D_FF], conv_w, conv_b)
    v = gv[..., D_FF:]
    return (jax.nn.silu(g) * v) @ w_down

def first_inputs(seed: int = 0) -> dict:
    key = jax.random.key(seed)
    ks = jax.random.split(key, 32)
    f32 = jnp.float32

    def nrm(k, shape, scale):
        return jax.random.normal(k, shape, f32) * scale

    def gain(k, shape):
        return 1.0 + 0.02 * jax.random.normal(k, shape, f32)

    L = DEPTH
    x = jax.random.normal(ks[0], (BATCH, SEQ, D_MODEL), f32)
    mem = jax.random.normal(ks[1], (BATCH, MEM_LEN, D_MODEL), f32)
    mix_norm_w = gain(ks[2], (L, D_MODEL))
    w_in = nrm(ks[3], (L, D_MODEL, IN_COLS), D_MODEL ** -0.5)
    n_idx = jnp.arange(S5_STATE, dtype=f32)
    s5_lambda_re = -0.5 + 0.01 * jax.random.normal(ks[4], (L, S5_GROUPS, S5_STATE), f32)
    s5_lambda_im = math.pi * n_idx + 0.01 * jax.random.normal(ks[5], (L, S5_GROUPS, S5_STATE), f32)
    s5_log_dt = jax.random.uniform(ks[6], (L, S5_GROUPS), f32, math.log(0.001), math.log(0.1))
    s5_b_re = nrm(ks[7], (L, S5_GROUPS, S5_STATE, S5_GROUP_DIM), (2 * S5_GROUP_DIM) ** -0.5)
    s5_b_im = nrm(ks[8], (L, S5_GROUPS, S5_STATE, S5_GROUP_DIM), (2 * S5_GROUP_DIM) ** -0.5)
    s5_c_re = nrm(ks[9], (L, S5_GROUPS, S5_GROUP_DIM, S5_STATE), S5_STATE ** -0.5)
    s5_c_im = nrm(ks[10], (L, S5_GROUPS, S5_GROUP_DIM, S5_STATE), S5_STATE ** -0.5)
    s5_d = nrm(ks[11], (L, S5_WIDTH), 1.0)
    s5_w_glu = nrm(ks[12], (L, S5_WIDTH, S5_WIDTH), S5_WIDTH ** -0.5)
    ssd_conv_w = nrm(ks[13], (L, SSD_CONV, SSD_CONV_DIM), SSD_CONV ** -0.5)
    ssd_conv_b = nrm(ks[14], (L, SSD_CONV_DIM), 0.01)
    dt0 = jnp.exp(jax.random.uniform(ks[15], (L, SSD_HEADS), f32, math.log(0.001), math.log(0.1)))
    ssd_dt_bias = dt0 + jnp.log(-jnp.expm1(-dt0))
    ssd_a_log = jnp.log(jax.random.uniform(ks[16], (L, SSD_HEADS), f32, 1.0, 16.0))
    ssd_d = gain(ks[17], (L, SSD_HEADS))
    ssd_norm_w = gain(ks[18], (L, SSD_INNER))
    w_out = nrm(ks[19], (L, MIX_WIDTH, D_MODEL), MIX_WIDTH ** -0.5)
    xa_norm_w = gain(ks[20], (L, D_MODEL))
    mem_norm_w = gain(ks[21], (L, D_MODEL))
    xa_wq = nrm(ks[22], (L, D_MODEL, D_MODEL), D_MODEL ** -0.5)
    xa_wk = nrm(ks[23], (L, D_MODEL, D_MODEL), D_MODEL ** -0.5)
    xa_wv = nrm(ks[24], (L, D_MODEL, D_MODEL), D_MODEL ** -0.5)
    xa_wo = nrm(ks[25], (L, D_MODEL, D_MODEL), D_MODEL ** -0.5)
    ffn_norm_w = gain(ks[26], (L, D_MODEL))
    ffn_w_up = nrm(ks[27], (L, D_MODEL, 2 * D_FF), D_MODEL ** -0.5)
    ffn_conv_w = nrm(ks[28], (L, FFN_CONV, D_FF), FFN_CONV ** -0.5)
    ffn_conv_b = nrm(ks[29], (L, D_FF), 0.01)
    ffn_w_down = nrm(ks[30], (L, D_FF, D_MODEL), D_FF ** -0.5)
    final_norm_w = gain(ks[31], (D_MODEL,))
    return {"x": x, "mem": mem, "mix_norm_w": mix_norm_w, "w_in": w_in,
            "s5_lambda_re": s5_lambda_re, "s5_lambda_im": s5_lambda_im, "s5_log_dt": s5_log_dt,
            "s5_b_re": s5_b_re, "s5_b_im": s5_b_im, "s5_c_re": s5_c_re, "s5_c_im": s5_c_im,
            "s5_d": s5_d, "s5_w_glu": s5_w_glu,
            "ssd_conv_w": ssd_conv_w, "ssd_conv_b": ssd_conv_b, "ssd_dt_bias": ssd_dt_bias,
            "ssd_a_log": ssd_a_log, "ssd_d": ssd_d, "ssd_norm_w": ssd_norm_w, "w_out": w_out,
            "xa_norm_w": xa_norm_w, "mem_norm_w": mem_norm_w, "xa_wq": xa_wq, "xa_wk": xa_wk,
            "xa_wv": xa_wv, "xa_wo": xa_wo, "ffn_norm_w": ffn_norm_w, "ffn_w_up": ffn_w_up,
            "ffn_conv_w": ffn_conv_w, "ffn_conv_b": ffn_conv_b, "ffn_w_down": ffn_w_down,
            "final_norm_w": final_norm_w}

def first_block(x, mem, mix_norm_w, w_in, s5_lambda_re, s5_lambda_im, s5_log_dt, s5_b_re, s5_b_im,
              s5_c_re, s5_c_im, s5_d, s5_w_glu, ssd_conv_w, ssd_conv_b, ssd_dt_bias, ssd_a_log,
              ssd_d, ssd_norm_w, w_out, xa_norm_w, mem_norm_w, xa_wq, xa_wk, xa_wv, xa_wo,
              ffn_norm_w, ffn_w_up, ffn_conv_w, ffn_conv_b, ffn_w_down, final_norm_w):
    c_u = S5_WIDTH
    c_z = c_u + SSD_INNER
    c_xbc = c_z + SSD_CONV_DIM
    for i in range(DEPTH):
        h = rmsnorm(x, mix_norm_w[i])
        proj = h @ w_in[i]
        y_s5 = s5_mixer(proj[..., :c_u], s5_lambda_re[i], s5_lambda_im[i], s5_log_dt[i],
                        s5_b_re[i], s5_b_im[i], s5_c_re[i], s5_c_im[i], s5_d[i], s5_w_glu[i])
        y_ssd = ssd_mixer(proj[..., c_u:c_z], proj[..., c_z:c_xbc], proj[..., c_xbc:],
                          ssd_conv_w[i], ssd_conv_b[i], ssd_dt_bias[i], ssd_a_log[i],
                          ssd_d[i], ssd_norm_w[i])
        x = x + jnp.concatenate([y_s5, y_ssd], axis=-1) @ w_out[i]
        h = rmsnorm(x, xa_norm_w[i])
        mem_n = rmsnorm(mem, mem_norm_w[i])
        x = x + cross_attention(h, mem_n, xa_wq[i], xa_wk[i], xa_wv[i], xa_wo[i])
        h = rmsnorm(x, ffn_norm_w[i])
        x = x + conv_ffn(h, ffn_w_up[i], ffn_conv_w[i], ffn_conv_b[i], ffn_w_down[i])
    return rmsnorm(x, final_norm_w)


DEPTH_2 = 2

N_MIXERS = 3
ROPE_THETA = 500000.0
BLOCK = 128
NEG_INF = -1e30
SWA_HEADS = 16
SWA_KV_HEADS = 4
SWA_HEAD_DIM = D_MODEL // SWA_HEADS
SWA_GROUP = SWA_HEADS // SWA_KV_HEADS
SWA_WINDOW = 128
SWA_ROT = SWA_HEAD_DIM // 4
RWKV_HEAD_DIM = 64
RWKV_HEADS = D_MODEL // RWKV_HEAD_DIM
RWKV_DECAY_LORA = 64
RWKV_A_LORA = 64
RWKV_GATE_LORA = 160
RWKV_GN_EPS = 64e-5
MLA_HEADS = 16
MLA_NOPE = 64
MLA_ROPE = 32
MLA_V = 64
MLA_Q_LORA = 384
MLA_KV_LORA = 256
FFN_DIM = 2816
CONV_WIDTH = 3


F32 = jnp.float32

def rms_norm(x, g):
    xf = x.astype(F32)
    y = xf * lax.rsqrt(jnp.mean(xf * xf, axis=-1, keepdims=True) + NORM_EPS)
    return (y * g.astype(F32)).astype(x.dtype)

def rope_tables(seq, rot_dim):
    inv = ROPE_THETA ** (-jnp.arange(0, rot_dim, 2, dtype=F32) / rot_dim)
    ang = jnp.arange(seq, dtype=F32)[:, None] * inv[None, :]
    return jnp.cos(ang), jnp.sin(ang)

def rope_slice(x, cos, sin, start):
    rot = 2 * cos.shape[-1]
    half = rot // 2
    x1 = x[..., start:start + half]
    x2 = x[..., start + half:start + rot]
    c = cos[None, :, None, :].astype(x.dtype)
    s = sin[None, :, None, :].astype(x.dtype)
    return jnp.concatenate([x[..., :start], x1 * c - x2 * s, x2 * c + x1 * s, x[..., start + rot:]], axis=-1)

def swa_mixer(h, w_qkv, q_gain, k_gain, sinks, w_o, cos, sin):
    b, s, _ = h.shape
    nb = s // BLOCK
    qd = SWA_HEADS * SWA_HEAD_DIM
    kd = SWA_KV_HEADS * SWA_HEAD_DIM
    qkv = h @ w_qkv
    q = qkv[..., :qd].reshape(b, s, SWA_HEADS, SWA_HEAD_DIM)
    k = qkv[..., qd:qd + kd].reshape(b, s, SWA_KV_HEADS, SWA_HEAD_DIM)
    v = qkv[..., qd + kd:].reshape(b, s, SWA_KV_HEADS, SWA_HEAD_DIM)
    q = rope_slice(rms_norm(q, q_gain), cos, sin, 0)
    k = rope_slice(rms_norm(k, k_gain), cos, sin, 0)
    q = q.reshape(b, nb, BLOCK, SWA_KV_HEADS, SWA_GROUP, SWA_HEAD_DIM)

    def band(t):
        tp = jnp.pad(t, ((0, 0), (BLOCK, BLOCK), (0, 0), (0, 0)))
        tp = tp.reshape(b, nb + 2, BLOCK, SWA_KV_HEADS, SWA_HEAD_DIM)
        return jnp.concatenate([tp[:, :-2], tp[:, 1:-1], tp[:, 2:]], axis=2)

    kb, vb = band(k), band(v)
    blk = jnp.arange(nb)[:, None]
    qpos = blk * BLOCK + jnp.arange(BLOCK)[None, :]
    kpos = (blk - 1) * BLOCK + jnp.arange(3 * BLOCK)[None, :]
    valid = ((kpos >= 0) & (kpos < s))[:, None, :]
    mask = (jnp.abs(qpos[:, :, None] - kpos[:, None, :]) <= SWA_WINDOW) & valid
    sink = sinks.astype(F32).reshape(SWA_KV_HEADS, SWA_GROUP)[None, :, :, None, None]
    scale = SWA_HEAD_DIM ** -0.5

    def attend(args):
        qb, kbb, vbb, mb = args
        sc = jnp.einsum('bqhgd,bkhd->bhgqk', qb, kbb).astype(F32) * scale
        sc = jnp.where(mb, sc, NEG_INF)
        m = jnp.maximum(jnp.max(sc, axis=-1, keepdims=True), sink)
        p = jnp.exp(sc - m)
        p = p / (jnp.sum(p, axis=-1, keepdims=True) + jnp.exp(sink - m))
        return jnp.einsum('bhgqk,bkhd->bqhgd', p.astype(vbb.dtype), vbb)

    o = lax.map(attend, (jnp.moveaxis(q, 1, 0), jnp.moveaxis(kb, 1, 0), jnp.moveaxis(vb, 1, 0), mask))
    o = jnp.moveaxis(o, 0, 1).reshape(b, s, qd)
    return o @ w_o

def wkv7_scan(r, w, k, v, a, bb, reverse):
    b, s, nh, n = r.shape
    seq = tuple(jnp.moveaxis(t, 1, 0) for t in (r, w, k, v, a, bb))

    def step(state, inp):
        r_t, w_t, k_t, v_t, a_t, b_t = inp
        sa = jnp.einsum('bhvk,bhk->bhv', state, a_t)
        state = state * w_t[:, :, None, :] + sa[..., None] * b_t[:, :, None, :] + v_t[..., None] * k_t[:, :, None, :]
        y = jnp.einsum('bhvk,bhk->bhv', state, r_t)
        return state, y

    s0 = jnp.zeros((b, nh, n, n), F32)
    _, y = lax.scan(step, s0, seq, reverse=reverse)
    return jnp.moveaxis(y, 0, 1)

def rwkv7_mixer(h, mu, w_r, w_k, w_v, w0, w1, w2, a0, a1, a2, g1, g2, k_k, k_a, r_k, lnx_w, lnx_b, w_o):
    b, s, d = h.shape
    hp = jnp.pad(h, ((0, 0), (1, 1), (0, 0)))
    xx = 0.5 * (hp[:, :-2] + hp[:, 2:]) - h
    xr = h + xx * mu[0]
    xw = h + xx * mu[1]
    xk = h + xx * mu[2]
    xv = h + xx * mu[3]
    xa = h + xx * mu[4]
    xg = h + xx * mu[5]
    r = xr @ w_r
    k = xk @ w_k
    v = xv @ w_v
    g = jax.nn.sigmoid(xg @ g1) @ g2

    def heads(t):
        return t.reshape(b, s, RWKV_HEADS, RWKV_HEAD_DIM)

    kk = heads(k * k_k).astype(F32)
    kk = kk / jnp.maximum(jnp.sqrt(jnp.sum(kk * kk, axis=-1, keepdims=True)), 1e-12)
    rf = heads(r).astype(F32)
    vf = heads(v).astype(F32)
    kf = k.astype(F32)
    rkf = r_k.astype(F32)

    def direction(dirn):
        wl = (w0[dirn] + jnp.tanh(xw @ w1[dirn]) @ w2[dirn]).astype(F32)
        decay = jnp.exp(-jnp.exp(-jax.nn.softplus(-wl) - 0.5))
        a = jax.nn.sigmoid((a0[dirn] + (xa @ a1[dirn]) @ a2[dirn]).astype(F32))
        kd = kf * (1.0 + (a - 1.0) * k_a.astype(F32))
        a, kd, decay = heads(a), heads(kd), heads(decay)
        y = wkv7_scan(rf, decay, kd, vf, -kk, kk * a, reverse=(dirn == 1))
        bonus = jnp.sum(rf * kd * rkf, axis=-1, keepdims=True) * vf
        return y, bonus

    y_f, bonus_f = direction(0)
    y_b, bonus_b = direction(1)
    y = y_f + y_b
    mean = jnp.mean(y, axis=-1, keepdims=True)
    var = jnp.mean(jnp.square(y - mean), axis=-1, keepdims=True)
    yn = ((y - mean) * lax.rsqrt(var + RWKV_GN_EPS)).reshape(b, s, d) * lnx_w.astype(F32) + lnx_b.astype(F32)
    out = (yn + (bonus_f + bonus_b).reshape(b, s, d)) * g.astype(F32)
    return out.astype(h.dtype) @ w_o

def mla_mixer(h, w_down, cq_gain, ckv_gain, w_uq, w_ukv, q_gain, k_gain, w_o, cos, sin):
    b, s, _ = h.shape
    nb = s // BLOCK
    down = h @ w_down
    cq = rms_norm(down[..., :MLA_Q_LORA], cq_gain)
    ckv = rms_norm(down[..., MLA_Q_LORA:MLA_Q_LORA + MLA_KV_LORA], ckv_gain)
    k_rope = down[..., MLA_Q_LORA + MLA_KV_LORA:]
    q = (cq @ w_uq).reshape(b, s, MLA_HEADS, MLA_NOPE + MLA_ROPE)
    kv = (ckv @ w_ukv).reshape(b, s, MLA_HEADS, MLA_NOPE + MLA_V)
    k = jnp.concatenate([kv[..., :MLA_NOPE], jnp.broadcast_to(k_rope[:, :, None, :], (b, s, MLA_HEADS, MLA_ROPE))], axis=-1)
    v = kv[..., MLA_NOPE:]
    q = rope_slice(rms_norm(q, q_gain), cos, sin, MLA_NOPE)
    k = rope_slice(rms_norm(k, k_gain), cos, sin, MLA_NOPE)
    scale = (MLA_NOPE + MLA_ROPE) ** -0.5
    qb = jnp.moveaxis(q.reshape(b, nb, BLOCK, MLA_HEADS, MLA_NOPE + MLA_ROPE), 1, 0)

    def attend(qblk):
        sc = jnp.einsum('bqhd,bkhd->bhqk', qblk, k).astype(F32) * scale
        p = jax.nn.softmax(sc, axis=-1)
        return jnp.einsum('bhqk,bkhd->bqhd', p.astype(v.dtype), v)

    o = lax.map(attend, qb)
    o = jnp.moveaxis(o, 0, 1).reshape(b, s, MLA_HEADS * MLA_V)
    return o @ w_o

def conv_ffn_2(h, w_up, conv_w, conv_b, w_down):
    s = h.shape[1]
    pad = CONV_WIDTH // 2
    u = h @ w_up
    up = jnp.pad(u, ((0, 0), (pad, pad), (0, 0)))
    acc = up[:, :s] * conv_w[0] + conv_b
    for t in range(1, CONV_WIDTH):
        acc = acc + up[:, t:t + s] * conv_w[t]
    gate, val = jnp.split(acc, 2, axis=-1)
    return (jax.nn.silu(gate) * val) @ w_down

def second_inputs(seed: int = 0) -> dict:
    key = jax.random.key(seed)
    ks = iter(jax.random.split(key, 48))
    n_a = len(range(0, DEPTH_2, N_MIXERS))
    n_b = len(range(1, DEPTH_2, N_MIXERS))
    n_c = len(range(2, DEPTH_2, N_MIXERS))
    d = D_MODEL

    def nrm(shape, scale):
        return scale * jax.random.normal(next(ks), shape, F32)

    def unif(shape, lo, hi):
        return jax.random.uniform(next(ks), shape, F32, lo, hi)

    qkv_w = (SWA_HEADS + 2 * SWA_KV_HEADS) * SWA_HEAD_DIM
    return {
        'x': nrm((BATCH, SEQ, d), 1.0),
        'norm_tok': 1.0 + nrm((DEPTH_2, d), 0.05),
        'norm_ch': 1.0 + nrm((DEPTH_2, d), 0.05),
        'ffn_w_up': nrm((DEPTH_2, d, 2 * FFN_DIM), d ** -0.5),
        'ffn_conv_w': nrm((DEPTH_2, CONV_WIDTH, 2 * FFN_DIM), CONV_WIDTH ** -0.5),
        'ffn_conv_b': nrm((DEPTH_2, 2 * FFN_DIM), 0.02),
        'ffn_w_down': nrm((DEPTH_2, FFN_DIM, d), FFN_DIM ** -0.5),
        'swa_w_qkv': nrm((n_a, d, qkv_w), d ** -0.5),
        'swa_q_gain': 1.0 + nrm((n_a, SWA_HEAD_DIM), 0.05),
        'swa_k_gain': 1.0 + nrm((n_a, SWA_HEAD_DIM), 0.05),
        'swa_sinks': nrm((n_a, SWA_HEADS), 1.0),
        'swa_w_o': nrm((n_a, SWA_HEADS * SWA_HEAD_DIM, d), d ** -0.5),
        'rwkv_mu': unif((n_b, 6, d), 0.0, 1.0),
        'rwkv_w_r': nrm((n_b, d, d), d ** -0.5),
        'rwkv_w_k': nrm((n_b, d, d), d ** -0.5),
        'rwkv_w_v': nrm((n_b, d, d), d ** -0.5),
        'rwkv_w0': unif((n_b, 2, d), -6.0, -1.0),
        'rwkv_w1': nrm((n_b, 2, d, RWKV_DECAY_LORA), d ** -0.5),
        'rwkv_w2': nrm((n_b, 2, RWKV_DECAY_LORA, d), 0.5 * RWKV_DECAY_LORA ** -0.5),
        'rwkv_a0': nrm((n_b, 2, d), 0.5),
        'rwkv_a1': nrm((n_b, 2, d, RWKV_A_LORA), d ** -0.5),
        'rwkv_a2': nrm((n_b, 2, RWKV_A_LORA, d), 0.5 * RWKV_A_LORA ** -0.5),
        'rwkv_g1': nrm((n_b, d, RWKV_GATE_LORA), d ** -0.5),
        'rwkv_g2': nrm((n_b, RWKV_GATE_LORA, d), RWKV_GATE_LORA ** -0.5),
        'rwkv_k_k': 0.85 + nrm((n_b, d), 0.1),
        'rwkv_k_a': 1.0 + nrm((n_b, d), 0.1),
        'rwkv_r_k': nrm((n_b, RWKV_HEADS, RWKV_HEAD_DIM), 0.1),
        'rwkv_lnx_w': 1.0 + nrm((n_b, d), 0.05),
        'rwkv_lnx_b': nrm((n_b, d), 0.01),
        'rwkv_w_o': nrm((n_b, d, d), d ** -0.5),
        'mla_w_down': nrm((n_c, d, MLA_Q_LORA + MLA_KV_LORA + MLA_ROPE), d ** -0.5),
        'mla_cq_gain': 1.0 + nrm((n_c, MLA_Q_LORA), 0.05),
        'mla_ckv_gain': 1.0 + nrm((n_c, MLA_KV_LORA), 0.05),
        'mla_w_uq': nrm((n_c, MLA_Q_LORA, MLA_HEADS * (MLA_NOPE + MLA_ROPE)), MLA_Q_LORA ** -0.5),
        'mla_w_ukv': nrm((n_c, MLA_KV_LORA, MLA_HEADS * (MLA_NOPE + MLA_V)), MLA_KV_LORA ** -0.5),
        'mla_q_gain': 1.0 + nrm((n_c, MLA_NOPE + MLA_ROPE), 0.05),
        'mla_k_gain': 1.0 + nrm((n_c, MLA_NOPE + MLA_ROPE), 0.05),
        'mla_w_o': nrm((n_c, MLA_HEADS * MLA_V, d), d ** -0.5),
    }

def second_block(x, norm_tok, norm_ch, ffn_w_up, ffn_conv_w, ffn_conv_b, ffn_w_down,
              swa_w_qkv, swa_q_gain, swa_k_gain, swa_sinks, swa_w_o,
              rwkv_mu, rwkv_w_r, rwkv_w_k, rwkv_w_v, rwkv_w0, rwkv_w1, rwkv_w2,
              rwkv_a0, rwkv_a1, rwkv_a2, rwkv_g1, rwkv_g2, rwkv_k_k, rwkv_k_a, rwkv_r_k,
              rwkv_lnx_w, rwkv_lnx_b, rwkv_w_o,
              mla_w_down, mla_cq_gain, mla_ckv_gain, mla_w_uq, mla_w_ukv,
              mla_q_gain, mla_k_gain, mla_w_o):
    s = x.shape[1]
    cos_a, sin_a = rope_tables(s, SWA_ROT)
    cos_c, sin_c = rope_tables(s, MLA_ROPE)
    for i in range(DEPTH_2):
        kind = i % N_MIXERS
        j = i // N_MIXERS
        h = rms_norm(x, norm_tok[i])
        if kind == 0:
            y = swa_mixer(h, swa_w_qkv[j], swa_q_gain[j], swa_k_gain[j], swa_sinks[j], swa_w_o[j], cos_a, sin_a)
        elif kind == 1:
            y = rwkv7_mixer(h, rwkv_mu[j], rwkv_w_r[j], rwkv_w_k[j], rwkv_w_v[j], rwkv_w0[j], rwkv_w1[j], rwkv_w2[j],
                            rwkv_a0[j], rwkv_a1[j], rwkv_a2[j], rwkv_g1[j], rwkv_g2[j], rwkv_k_k[j], rwkv_k_a[j],
                            rwkv_r_k[j], rwkv_lnx_w[j], rwkv_lnx_b[j], rwkv_w_o[j])
        else:
            y = mla_mixer(h, mla_w_down[j], mla_cq_gain[j], mla_ckv_gain[j], mla_w_uq[j], mla_w_ukv[j],
                          mla_q_gain[j], mla_k_gain[j], mla_w_o[j], cos_c, sin_c)
        x = x + y
        x = x + conv_ffn_2(rms_norm(x, norm_ch[i]), ffn_w_up[i], ffn_conv_w[i], ffn_conv_b[i], ffn_w_down[i])
    return x


def setup_inputs(seed=0):
    out = dict(first_inputs(seed))
    for name, value in second_inputs(seed + 1).items():
        if name != "x":
            out[name + "_2"] = value
    return out


def reference(
    x, mem, mix_norm_w, w_in, s5_lambda_re, s5_lambda_im, s5_log_dt, s5_b_re, s5_b_im, s5_c_re,
    s5_c_im, s5_d, s5_w_glu, ssd_conv_w, ssd_conv_b, ssd_dt_bias, ssd_a_log, ssd_d, ssd_norm_w,
    w_out, xa_norm_w, mem_norm_w, xa_wq, xa_wk, xa_wv, xa_wo, ffn_norm_w, ffn_w_up, ffn_conv_w,
    ffn_conv_b, ffn_w_down, final_norm_w, norm_tok_2, norm_ch_2, ffn_w_up_2, ffn_conv_w_2,
    ffn_conv_b_2, ffn_w_down_2, swa_w_qkv_2, swa_q_gain_2, swa_k_gain_2, swa_sinks_2, swa_w_o_2,
    rwkv_mu_2, rwkv_w_r_2, rwkv_w_k_2, rwkv_w_v_2, rwkv_w0_2, rwkv_w1_2, rwkv_w2_2, rwkv_a0_2,
    rwkv_a1_2, rwkv_a2_2, rwkv_g1_2, rwkv_g2_2, rwkv_k_k_2, rwkv_k_a_2, rwkv_r_k_2,
    rwkv_lnx_w_2, rwkv_lnx_b_2, rwkv_w_o_2, mla_w_down_2, mla_cq_gain_2, mla_ckv_gain_2,
    mla_w_uq_2, mla_w_ukv_2, mla_q_gain_2, mla_k_gain_2, mla_w_o_2,
):
    x = first_block(
        x, mem, mix_norm_w, w_in, s5_lambda_re, s5_lambda_im, s5_log_dt, s5_b_re, s5_b_im,
        s5_c_re, s5_c_im, s5_d, s5_w_glu, ssd_conv_w, ssd_conv_b, ssd_dt_bias, ssd_a_log, ssd_d,
        ssd_norm_w, w_out, xa_norm_w, mem_norm_w, xa_wq, xa_wk, xa_wv, xa_wo, ffn_norm_w,
        ffn_w_up, ffn_conv_w, ffn_conv_b, ffn_w_down, final_norm_w,
    )
    return second_block(
        x, norm_tok_2, norm_ch_2, ffn_w_up_2, ffn_conv_w_2, ffn_conv_b_2, ffn_w_down_2,
        swa_w_qkv_2, swa_q_gain_2, swa_k_gain_2, swa_sinks_2, swa_w_o_2, rwkv_mu_2, rwkv_w_r_2,
        rwkv_w_k_2, rwkv_w_v_2, rwkv_w0_2, rwkv_w1_2, rwkv_w2_2, rwkv_a0_2, rwkv_a1_2,
        rwkv_a2_2, rwkv_g1_2, rwkv_g2_2, rwkv_k_k_2, rwkv_k_a_2, rwkv_r_k_2, rwkv_lnx_w_2,
        rwkv_lnx_b_2, rwkv_w_o_2, mla_w_down_2, mla_cq_gain_2, mla_ckv_gain_2, mla_w_uq_2,
        mla_w_ukv_2, mla_q_gain_2, mla_k_gain_2, mla_w_o_2,
    )


_drawn_inputs = setup_inputs


def setup_inputs(seed=0):
    import zlib

    import numpy as np

    out = dict(_drawn_inputs(seed))
    spreads = {}
    factors = {'s5_lambda_re': 200.0,
     's5_lambda_im': 3.067,
     's5_log_dt': 3.193,
     's5_b_re': 4.183,
     's5_b_im': 4.206,
     's5_c_re': 4.318,
     's5_c_im': 4.279,
     'ssd_conv_b': 3.603,
     'ssd_d': 4.634,
     'ssd_norm_w': 2.705,
     'xa_norm_w': 8.0,
     'mem_norm_w': 8.0,
     'ffn_norm_w': 3.228,
     'ffn_conv_b': 8.0,
     'swa_q_gain_2': 7.111,
     'swa_k_gain_2': 7.47,
     'swa_sinks_2': 8.0,
     'rwkv_w1_2': 4.171,
     'rwkv_w2_2': 4.148,
     'rwkv_lnx_b_2': 24.393,
     'ffn_conv_b_2': 3.328,
     'rwkv_lnx_w_2': 3.202}
    for name, (base, spread) in spreads.items():
        noise = np.random.default_rng([zlib.crc32(name.encode()), seed]).standard_normal(out[name].shape)
        drawn = base * np.exp(spread * noise) if base else spread * noise
        out[name] = __import__('jax').numpy.asarray(drawn.astype(out[name].dtype))
    for name, factor in factors.items():
        out[name] = (out[name] * factor).astype(out[name].dtype)
    return out
```

```python
import math
from contextlib import ExitStack

import concourse.bass as bass
import numpy as np
from concourse import mybir

D = 1024
T = 256
P = 128
TT = T // P
KB = D // P
S5_W, S5_TILES = 256, 8
INNER, HEADS, GROUPS = 768, 12, 4
HPG = HEADS // GROUPS
XB = INNER // P
CONVB = 14
FB = 22
XA_H = 4
SWA_H, SWA_KV, HD = 16, 4, 64
HALF_ROT = 8
EPS = 1e-6
GN_EPS = 64e-5
DECAY = math.exp(-0.5)

CHUNK = 4096
RING = 3
CHUNKS = [("w_in", 6), ("xa_k", 2), ("xa_v", 2), ("w_out", 2), ("xa_q", 2), ("xa_o", 2),
          ("up0", 11), ("down0", 6), ("qkv", 3), ("swa_o", 2), ("up1", 11), ("down1", 6),
          ("rw_r", 2), ("rw_k", 2), ("rw_v", 2), ("lora1", 1), ("lora2", 1), ("rw_o", 2),
          ("up2", 11), ("down2", 6)]
FIRST_CHUNK, _n = {}, 0
for _name, _count in CHUNKS:
    FIRST_CHUNK[_name] = _n
    _n += _count
N_CHUNKS = _n

BANKS = 8
LEVELS = 7


BATCHES = [[f"{d}{order}{half}" for order in (0, 1) for half in (0, 1)] for d in range(2)]


def _groups():
    out = [("tx_mix", 4), ("tx_mem", 4), ("xbc", 7), ("dt", 1), ("u", 1), ("z", 4),
           ("s5_bu", S5_TILES), ("xa_k", 4), ("acs", 1), ("xa_v", 4), ("cb", 2), ("x_tok", 3), ("b_tok", 1), ("state", 2), ("s5_y", 1), ("s5_glu", 1),
           ("row0", 4), ("diag0", 2), ("row1", 4), ("diag1", 2), ("off", 2), ("tx_ssd", 3),
           ("w_out", 4), ("tx_xa", 4), ("xa_q", 4)]
    out += [(f"xa_s{h}", 1) for h in range(XA_H)]
    out += [x for h in range(XA_H) for x in ((f"xa_t{h}", 1), (f"xa_ov{h}", 1))]
    out += [("xa_o", 4), ("tx_ffn0", 4), ("up0", 22), ("down0", 4),
            ("tx_swa", 4), ("qkv", 6), ("q_tr", 4), ("k_tr", 1)]
    out += [("sw_s0", 4)]
    for q in range(4):
        out += [(f"sw_s{q + 1}", 4)] * (q < 3) + [(f"sw_t{q}", 4), (f"sw_ov{q}", 1)]
    out += [("swa_o", 4), ("tx_ffn1", 4), ("up1", 22), ("down1", 4),
            ("tx_rw", 4), ("rw_r", 4), ("rw_k", 4), ("rw_v", 4), ("kk_ss", 1), ("lora1", 2), ("kk_bc", 4)]
    for d in range(2):
        out += [(f"wl0_{q}", 1) for q in range(4)] * (d == 0) + [(f"al{d}", 4), (f"bonus{d}", 1), (f"bk_tok{d}", 4)]
        out += [(f"ab{BATCHES[d][0]}_{j}", 1) for j in range(8)]
        for b, following in zip(BATCHES[d], BATCHES[d][1:] + [None]):
            for l in range(1, LEVELS):
                out += [(f"lv{l}_{b}", 6)]
                if following and l <= 4:
                    out += [(f"ab{following}_{j}", 1) for j in (2 * l - 2, 2 * l - 1)]
                if d == 0 and not following and l <= 4:
                    out += [(f"wl1_{l - 1}", 1)]
            out += [("xs" + b, 1), ("us" + b, 1), ("ys" + b, 1)]
            if b[1] == "0":
                out += [("ss" + b, 1)]
    out += [("gate", 4), ("tx_y", 4), ("rw_o", 4), ("tx_ffn2", 4), ("up2", 22), ("down2", 4)]
    return out


G, _n = {}, 0
for _name, _count in _groups():
    G[_name] = _n
    _n += _count


def level_groups(lv, b, g):
    base = G[f"lv{lv}_{b}"]
    return (base + 2 + g, base + g, base + 4 + g) if lv == 1 else (base + 2 * g, base + 2 * g + 1, base + 4 + g)


def chunk_last_group():
    last = {}

    def put(name, ends):
        for i, e in enumerate(ends):
            last[FIRST_CHUNK[name] + i] = e

    x = G["xbc"]
    put("w_in", [x + 1, x + 3, x + 5, G["dt"], G["z"] + 1, G["z"] + 3])
    for name in ("xa_k", "xa_v", "w_out", "xa_q", "xa_o", "swa_o", "rw_r", "rw_k", "rw_v", "rw_o"):
        put(name, [G[name] + 1, G[name] + 3])
    put("qkv", [G["qkv"] + 1, G["qkv"] + 3, G["qkv"] + 5])
    for i in range(3):
        put(f"up{i}", [G[f"up{i}"] + 2 * c + 1 for c in range(11)])
        put(f"down{i}", [None] * 5 + [G[f"down{i}"] + 3])
    put("lora1", [G["lora1"] + 1])
    put("lora2", [G["gate"] + 3])
    return last


CHUNK_LAST = chunk_last_group()

COLS = [("mix_norm", 8), ("lam_re", 8), ("lam_im", 8), ("log_dt", 8), ("s5_d", 2),
        ("conv_w", 4 * CONVB), ("conv_b", CONVB), ("ssd_norm", XB), ("xa_norm", 8), ("mem_norm", 8),
        ("ffn_norm0", 8), ("ffn_norm1", 8), ("ffn_norm2", 8), ("tok_norm0", 8), ("tok_norm1", 8),
        ("fcw0", 3 * FB), ("fcb0", FB), ("fcw1", 6 * FB), ("fcb1", 2 * FB),
        ("fcw2", 6 * FB), ("fcb2", 2 * FB),
        ("mu", 48), ("w0", 16), ("a0", 16), ("k_k", 8), ("k_a", 8), ("r_k", 8)]
COL, _n = {}, 0
for _name, _count in COLS:
    COL[_name] = _n
    _n += _count
N_COLS = _n

ROWS = [("dt_bias", HEADS), ("a_log", HEADS), ("ssd_d", HEADS), ("sinks", SWA_H),
        ("q_gain", HD), ("k_gain", HD)]
ROW, _n = {}, 0
for _name, _count in ROWS:
    ROW[_name] = _n
    _n += _count
N_ROWS = _n

CST = [("ident", P), ("tri", P), ("ones", P), ("maskneg", P), ("headsel", KB * 16),
       ("keep0", T), ("keep1", T)]
CS, _n = {}, 0
for _name, _count in CST:
    CS[_name] = _n
    _n += _count
N_CST = _n
SWC = {"mask": 0, "cos": TT * T, "sin": TT * T + TT * HALF_ROT}
N_SWC = TT * T + 2 * TT * HALF_ROT
MSK_DIR = 256 + LEVELS * 256


def pair_order():
    return [h for g in (0, 2) for i in range(4) for h in (4 * g + i, 4 * g + 4 + i)]


def constants():
    c = np.zeros((P, N_CST), np.float32)
    s, l = np.arange(P)[:, None], np.arange(P)[None, :]
    c[:, CS["ident"]:][:, :P] = s == l
    c[:, CS["tri"]:][:, :P] = s <= l
    c[:, CS["ones"]:][:, :P] = 1.0
    c[:, CS["maskneg"]:][:, :P] = np.where(l >= s, 0.0, -1e30)
    sel = np.zeros((P, KB, 16), np.float32)
    for fb in range(KB):
        for p in range(P):
            sel[p, fb, 2 * fb + p // HD] = 1.0
    c[:, CS["headsel"]:][:, :KB * 16] = sel.reshape(P, -1)
    q, k = np.arange(T)[:, None], np.arange(T)[None, :]
    m = np.where(np.abs(q - k) <= 128, 3e38, -1e30).astype(np.float32)
    sw = np.zeros((P, N_SWC), np.float32)
    sw[:, SWC["mask"]:][:, :TT * T] = m.reshape(TT, P, T).transpose(1, 0, 2).reshape(P, -1)
    inv = np.float32(500000.0) ** (-np.arange(0, 16, 2, dtype=np.float32) / np.float32(16))
    ang = np.arange(T, dtype=np.float32)[:, None] * inv[None, :]
    for name, f in (("cos", np.cos), ("sin", np.sin)):
        sw[:, SWC[name]:][:, :TT * HALF_ROT] = f(ang).reshape(TT, P, HALF_ROT).transpose(1, 0, 2).reshape(P, -1)
    c[:, CS["keep0"]:][:, :T] = np.arange(T) % P != 0
    c[:, CS["keep1"]:][:, :T] = np.arange(T) % P != P - 1
    masks = np.zeros((P, 2, MSK_DIR), np.float32)
    for d in range(2):
        later = (lambda a, b: a > b) if d == 0 else (lambda a, b: a < b)
        masks[:, d, 0:P] = later(l, s)
        masks[:, d, P:2 * P] = later(l, s) | (l == s)
        for v in range(LEVELS):
            b = 1 << v
            off = (s // (2 * b) == l // (2 * b)) & (s // b != l // b) & later(s, l)
            masks[:, d, 256 + 256 * v:][:, :P] = off
            masks[:, d, 256 + 256 * v:][:, P:2 * P] = off.T
    back = sel.transpose(2, 1, 0).reshape(16, KB * P)
    return c, sw, masks.reshape(P, 2 * MSK_DIR), np.ascontiguousarray(back)


def by_columns(w):
    n = -(-w.shape[1] // 512)
    full = np.zeros((D, n * 512), np.float32)
    full[:, :w.shape[1]] = w
    return full.reshape(KB, P, n, 512).transpose(2, 1, 0, 3).reshape(n, P, CHUNK)


def by_rows(w):
    full = np.zeros((24 * P, D), np.float32)
    full[:w.shape[0]] = w
    return full.reshape(6, 4, P, D).transpose(0, 2, 1, 3).reshape(6, P, CHUNK)


def up_pairs(w):
    gate, value = w[:, :FB * P], w[:, FB * P:]
    cols = [part[:, c * 256:(c + 1) * 256] for c in range(FB // 2) for part in (gate, value)]
    return by_columns(np.concatenate(cols, axis=1))


def columns(v):
    return np.asarray(v).reshape(-1, P).T


def lay_out(i):
    w = i["w_in"][0]
    u, z, xbc, dt = w[:, :256], w[:, 256:1024], w[:, 1024:2816], w[:, 2816:2828]
    tail = np.zeros((D, 256), np.float32)
    tail[:, :HEADS] = dt
    heads = pair_order()
    qkv = i["swa_w_qkv_2"][0]
    q = qkv[:, :D].reshape(D, SWA_H, HD)[:, heads].reshape(D, D)
    lora1 = np.concatenate([i["rwkv_w1_2"][0, 0], i["rwkv_w1_2"][0, 1], i["rwkv_a1_2"][0, 0],
                            i["rwkv_a1_2"][0, 1], i["rwkv_g1_2"][0]], axis=1)
    lora2 = np.zeros((P, 4, D), np.float32)
    lora2[:, 0] = i["rwkv_w2_2"][0].reshape(P, D)
    lora2[:, 1] = i["rwkv_a2_2"][0].reshape(P, D)
    lora2[:, 2] = i["rwkv_g2_2"][0, :P]
    lora2[:32, 3] = i["rwkv_g2_2"][0, P:]
    parts = {
        "w_in": by_columns(np.concatenate([xbc, tail, u, z], axis=1)),
        "xa_k": by_columns(i["xa_wk"][0]), "xa_v": by_columns(i["xa_wv"][0]),
        "w_out": by_columns(i["w_out"][0]), "xa_q": by_columns(i["xa_wq"][0]),
        "xa_o": by_columns(i["xa_wo"][0]),
        "up0": up_pairs(i["ffn_w_up"][0]), "down0": by_rows(i["ffn_w_down"][0]),
        "qkv": by_columns(np.concatenate([q, qkv[:, D:]], axis=1)),
        "swa_o": by_columns(i["swa_w_o_2"][0].reshape(SWA_H, HD, D)[heads].reshape(D, D)),
        "up1": up_pairs(i["ffn_w_up_2"][0]), "down1": by_rows(i["ffn_w_down_2"][0]),
        "rw_r": by_columns(i["rwkv_w_r_2"][0]), "rw_k": by_columns(i["rwkv_w_k_2"][0]),
        "rw_v": by_columns(i["rwkv_w_v_2"][0]), "lora1": by_columns(lora1),
        "lora2": lora2.reshape(1, P, CHUNK), "rw_o": by_columns(i["rwkv_w_o_2"][0]),
        "up2": up_pairs(i["ffn_w_up_2"][1]), "down2": by_rows(i["ffn_w_down_2"][1]),
    }
    wall = np.concatenate([parts[name] for name, _ in CHUNKS], axis=0)

    def states(v):
        return np.asarray(v).reshape(S5_TILES, P).T

    log_dt = np.broadcast_to(i["s5_log_dt"][0][:, None], (16, 64))
    cols = [columns(i["mix_norm_w"][0]), states(i["s5_lambda_re"][0]), states(i["s5_lambda_im"][0]),
            states(log_dt), columns(i["s5_d"][0]), columns(i["ssd_conv_w"][0]), columns(i["ssd_conv_b"][0]),
            columns(i["ssd_norm_w"][0]), columns(i["xa_norm_w"][0]), columns(i["mem_norm_w"][0]),
            columns(i["ffn_norm_w"][0]), columns(i["norm_ch_2"][0]), columns(i["norm_ch_2"][1]),
            columns(i["norm_tok_2"][0]), columns(i["norm_tok_2"][1]),
            columns(i["ffn_conv_w"][0]), columns(i["ffn_conv_b"][0]),
            columns(i["ffn_conv_w_2"][0]), columns(i["ffn_conv_b_2"][0]),
            columns(i["ffn_conv_w_2"][1]), columns(i["ffn_conv_b_2"][1]),
            columns(i["rwkv_mu_2"][0]), columns(i["rwkv_w0_2"][0]), columns(i["rwkv_a0_2"][0]),
            columns(i["rwkv_k_k_2"][0]), columns(i["rwkv_k_a_2"][0]), columns(i["rwkv_r_k_2"][0])]
    prm = np.concatenate(cols, axis=1)
    rows = np.concatenate([i["ssd_dt_bias"][0], i["ssd_a_log"][0], i["ssd_d"][0],
                           i["swa_sinks_2"][0][heads], i["swa_q_gain_2"][0], i["swa_k_gain_2"][0]])[None, :]
    wide = np.stack([i["final_norm_w"], i["rwkv_lnx_w_2"][0], i["rwkv_lnx_b_2"][0]])
    b = np.zeros((P, 2, 2, P), np.float32)
    c = np.zeros((P, 2, S5_TILES, 32), np.float32)
    for r, (bm, cm) in enumerate((("s5_b_re", "s5_c_re"), ("s5_b_im", "s5_c_im"))):
        for g in range(16):
            j, loc = g // 2, g % 2
            row = 32 * (j % 4) + 16 * loc
            b[row:row + 16, r, j // 4, 64 * loc:64 * loc + 64] = i[bm][0, g].T
            c[64 * loc:64 * loc + 64, r, j, 16 * loc:16 * loc + 16] = i[cm][0, g].T
    glu = i["s5_w_glu"][0].reshape(2, P, S5_W).transpose(1, 0, 2).reshape(P, 2 * S5_W)
    cst, swc, masks, back = constants()
    tok = lambda a: a.reshape(TT, P, D).transpose(1, 0, 2).reshape(P, TT * D)
    out = {"x_tok": tok(i["x"][0]), "mem_tok": tok(i["mem"][0]), "wall": wall, "prm": prm, "rows": rows,
           "wide": wide, "s5b": b.reshape(P, -1), "s5c": c.reshape(P, -1), "glu": glu,
           "cst": cst, "swc": swc, "masks": masks, "back": back}
    return {k: np.ascontiguousarray(v) for k, v in out.items()}


NORM_AT = {0: 1, 1: 3, 2: 5, 3: 7, 5: 9, 6: 11, 7: 13, 8: 15}
RSTD_AT = {k: 2 * k + 1 for k in range(9)}
SUMSQ_AT = RSTD_AT
BATCH_AT = {(d, order, half): 4 * d + 2 * order + half for d in (0, 1) for order in (0, 1) for half in (0, 1)}


F32 = mybir.dt.float32
U8 = mybir.dt.uint8
ALU = mybir.AluOpType
ACT = mybir.ActivationFunctionType
AX = mybir.AxisListType.X
NORMS = ["mix", "mem", "xa", "ffn0", "final", "swa", "ffn1", "rw", "ffn2"]


def spread(ap, n):
    return ap.unsqueeze(2).to_broadcast([ap.shape[0], ap.shape[1], n])


def tiled(ap, n):
    return ap.unsqueeze(1).to_broadcast([ap.shape[0], n, ap.shape[1]])


def build(nc, io):
    ctx = ExitStack()
    with ctx:
        def sb(name, n, dt=F32):
            return ctx.enter_context(nc.sbuf_tensor(name, [P, n], dt))

        def sem(name):
            return ctx.enter_context(nc.semaphore(name))

        ring = sb("weight_ring", RING * CHUNK)[:, :].rearrange("p (s n) -> p s n", s=RING)
        x = sb("x", TT * D)[:, :].rearrange("p (t d) -> p t d", t=TT)
        hT_flat = sb("hT", KB * (T + 2))
        hT = hT_flat[:, :].rearrange("p (k t) -> p k t", k=KB)
        h_mid = hT[:, :, 1:T + 1]
        xn_flat = sb("xn", TT * D)
        xn = xn_flat[:, :].rearrange("p (t d) -> p t d", t=TT)
        cst = sb("cst", N_CST)
        masks = sb("masks", 2 * MSK_DIR, U8)
        prm = sb("prm", N_COLS)
        rows = sb("rows", N_ROWS)
        small = sb("small", 900)
        ARENA = 30720
        arena = sb("arena", ARENA)
        bank = [ctx.enter_context(nc.psum_tensor(f"bank{i}", [P, 512], F32)) for i in range(BANKS)]

        def carve(start, *sizes):
            out = []
            for n in sizes:
                assert start + n <= ARENA, (start, n)
                out.append(arena[:, start:start + n])
                start += n
            return out

        used_small = [0]

        def tiny(n):
            used_small[0] += n
            assert used_small[0] <= 900
            return small[:, used_small[0] - n:used_small[0]]

        def c_(name, n):
            return cst[:, CS[name]:CS[name] + n]

        def col(name, k=0, n=1):
            return prm[:, COL[name] + k:COL[name] + k + n]

        def row(name, n, k=0):
            return rows[:, ROW[name] + k:ROW[name] + k + n]

        ident = c_("ident", P)

        psum_full = sem("psum_full")
        bank_read = [sem(f"bank{i}_read") for i in range(BANKS)]
        chunk_in = [sem(f"chunk_in{i}") for i in range(RING)]

        def bank_sem(n):
            return bank_read[n % BANKS]

        def when_read(n):
            return bank_read[n % BANKS], n // BANKS + 1

        in_x = sem("in_x")
        down_chunk_used = sem("down_chunk_used")
        x_final_norm = sem("x_final_norm")
        out_done = sem("out_done")
        sumsq = sem("sumsq")
        in_mem = sem("in_mem")
        in_prm = sem("in_prm")
        s5_lrdt = sem("s5_lrdt")
        s5_angle = sem("s5_angle")
        xc_ready = sem("xc_ready")
        halved = sem("halved")
        dt_neg = sem("dt_neg")
        in_rows = sem("in_rows")
        acs_sub = sem("acs_sub")
        s5_gelu_in = sem("s5_gelu_in")
        y_gated = sem("y_gated")
        ssd_sumsq = sem("ssd_sumsq")
        xa_max = sem("xa_max")
        act_ready = sem("act_ready")
        qk_sums = sem("qk_sums")
        sw_max = sem("sw_max")
        masks_made = sem("masks_made")
        cum_done = sem("cum_done")
        y_centred = sem("y_centred")
        s5_dt = sem("s5_dt")
        s5_mag = sem("s5_mag")
        s5_trig = sem("s5_trig")
        xc_tanh = sem("xc_tanh")
        xc_tap = sem("xc_tap")
        z_tanh = sem("z_tanh")
        dt_ln = sem("dt_ln")
        decays = sem("decays")
        s5_gelu_tanh = sem("s5_gelu_tanh")
        lc_exp = sem("lc_exp")
        gate_tap = sem("gate_tap")
        value_tap = sem("value_tap")
        gate_tanh = sem("gate_tanh")
        qk_square = sem("qk_square")
        sw_exp = sem("sw_exp")
        rw_k_copied = sem("rw_k_copied")
        kk_square = sem("kk_square")
        e_up = sem("e_up")
        e_down = sem("e_down")
        e_before = sem("e_before")
        e_state = sem("e_state")
        gn_square = sem("gn_square")
        in_cst = sem("in_cst")
        in_s5b = sem("in_s5b")
        in_s5c = sem("in_s5c")
        in_glu = sem("in_glu")
        in_fnw = sem("in_fnw")
        in_swc = sem("in_swc")
        in_back = sem("in_back")
        in_masks = sem("in_masks")
        in_lnx = sem("in_lnx")
        act_step = sem("act_step")
        normed = sem("normed")
        da_ready = sem("da_ready")
        xdt_ready = sem("xdt_ready")
        s5_cw = sem("s5_cw")
        s5_h = sem("s5_h")
        s5_gelu = sem("s5_gelu")
        trid_ready = sem("trid_ready")
        lc_ready = sem("lc_ready")
        y_normed = sem("y_normed")
        s5_done = sem("s5_done")
        xa_p = sem("xa_p")
        roped = sem("roped")
        sw_p = sem("sw_p")
        x_mixed = sem("x_mixed")
        kk_rnorm = sem("kk_rnorm")
        rks_ready = sem("rks_ready")
        abkr_ready = sem("abkr_ready")
        b_scaled = sem("b_scaled")
        t_start = sem("t_start")
        gate_sigmoid = sem("gate_sigmoid")
        rstd_ready = sem("rstd_ready")
        s5_unit = sem("s5_unit")
        s5_table = sem("s5_table")
        ssd_rstd = sem("ssd_rstd")
        qk_rstd = sem("qk_rstd")
        la_zero = sem("la_zero")
        l_zero = sem("l_zero")
        t_identity = sem("t_identity")
        gn_rstd = sem("gn_rstd")
        constants_made = sem("constants_made")
        s5_scanned = sem("s5_scanned")
        gn_sums = sem("gn_sums")
        dve_step = sem("dve_step")
        pool_step = sem("pool_step")

        def b_(n, width=512):
            return bank[n % BANKS][:, 0:width]

        def b3(n, a, w):
            return bank[n % BANKS][:, 0:a * w].rearrange("p (a w) -> p a w", a=a)

        kT, v_xa, xc, xdt, xdtd, prevT, Lc, cb, triD, thA = carve(
            0, 2048, 2048, CONVB * T, 1536, 768, 768, 4 * 384, 1024, 768, 1024)
        uT, E, s5t, y5T, s5b, s5c, cw, yT = carve(15104, 512, 4096, 4608, 512, 512, 512, 512, 1536)
        y5g = thA
        y_ssd, = carve(27904, 1536)
        kT = kT.rearrange("p (k t) -> p k t", k=KB)
        v_xa = v_xa.rearrange("p (t d) -> p t d", t=TT)
        xc = xc.rearrange("p (k t) -> p k t", k=CONVB)
        memraw = s5t[:, 0:2048].rearrange("p (t d) -> p t d", t=TT)
        mem_junk = s5t[:, 2048:3072]
        memT = carve(26368, 2048)[0].rearrange("p (k t) -> p k t", k=KB)
        yT = yT.rearrange("p (k t) -> p k t", k=XB)
        xtok = hT_flat[:, 0:1536].rearrange("p (t d) -> p t d", t=TT)
        btok = hT_flat[:, 1536:2048]
        zs = xn_flat[:, 0:1536].rearrange("p (t d) -> p t d", t=TT)
        y_t = y_ssd.rearrange("p (t d) -> p t d", t=TT)
        xdt_t = xdt.rearrange("p (t d) -> p t d", t=TT)
        uT3 = uT.rearrange("p (k t) -> p k t", k=2)
        y5T3 = y5T.rearrange("p (k t) -> p k t", k=2)
        Er = E[:, 0:2048].rearrange("p (j t) -> p j t", j=S5_TILES)
        Ei = E[:, 2048:4096].rearrange("p (j t) -> p j t", j=S5_TILES)
        sp1, sp2, sgin = s5t[:, 0:512], s5t[:, 512:1024], s5t[:, 1024:1536]
        sgs = [s5t[:, 1536:2048], s5t[:, 2048:2560]]
        sq1, sq2 = s5t[:, 2560:3072], s5t[:, 3072:3584]
        glu = xn_flat[:, 1536:2048]
        qT, p_xa, pT_xa, oT = carve(4096, 2048, XA_H * 512, 1024, 2048)
        qT = qT.rearrange("p (k t) -> p k t", k=KB)
        oT = oT.rearrange("p (k t) -> p k t", k=KB)
        actT, f_acc, f_th, f_val = carve(8192, FB * T, 2 * 512, 2 * 512, 2 * 512)
        actT = actT.rearrange("p (k t) -> p k t", k=FB)
        fnw = carve(0, D)[0]
        swc = carve(29000, N_SWC)[0]
        qkv, w_sq, w_qT, w_kT, w_sc, w_p, w_pT, w_oT = carve(
            0, 3072, 1280, 2048, 512, 8 * 512, 8 * 512, 4 * 512, 2048)
        qkv = qkv.rearrange("p (t d) -> p t d", t=TT)
        w_qT = w_qT.rearrange("p (k t) -> p k t", k=KB)
        w_kT = w_kT.rearrange("p (k t) -> p k t", k=2)
        w_oT = w_oT.rearrange("p (k t) -> p k t", k=KB)
        (r_v, r_y, r_rT, r_kT, r_kk, r_AR, r_bh, r_kh, r_bk, r_LA, r_LB, r_TT, r_Yb, r_X, r_U, r_S,
         r_low, r_sg) = carve(0, 2048, 2048, 2048, 2048, 2048, 4096, 2048, 2048, 2048, 2048, 2048, 2048,
                              1024, 512, 512, 1024, 512, 512)
        r_vt = r_v.rearrange("p (t d) -> p t d", t=TT)
        r_yt = r_y.rearrange("p (t d) -> p t d", t=TT)
        three = lambda ap: ap.rearrange("p (k t) -> p k t", k=KB)
        r_rT3, r_kT3, r_kk3, r_bh3, r_kh3 = map(three, (r_rT, r_kT, r_kk, r_bh, r_kh))
        r_AR5 = r_AR.rearrange("p (k i a t) -> p k i a t", k=KB, i=TT, a=2)
        r_S4 = r_S.rearrange("p (k s c) -> p k s c", k=KB, s=2)
        x_mix = [three(r_AR[:, 0:2048]), three(r_AR[:, 2048:4096])]
        x_diff = three(r_bh)
        per_head = lambda ap: ap.rearrange("p (k o c) -> p k o c", k=8, o=2)
        r_Tk = per_head(r_TT)
        LAs, LBs = (hT_flat[:, 0:2048], r_LA), (xn_flat[:, :], r_LB)
        masks_in = carve(20480, 4096)[0]
        back = r_kh[0:16, 0:KB * P]
        hflat = hT_flat[:, 0:2048]
        lnx = r_LA
        r_oT = three(r_kh)

        ss = tiny(2 * len(NORMS))
        rs = tiny(2 * len(NORMS))
        rstd = tiny(2 * len(NORMS))
        mhalf = tiny(1)
        s_lr, s_dt, s_lrdt, s_th, s_k, s_r, s_abs, s_mag, s_sin, s_cos = [tiny(8) for _ in range(10)]
        s_abr, s_abi, s_den, s_fr, s_fi, s_t1, s_t2, s_pr, s_pi, s_nsin = [tiny(8) for _ in range(10)]
        s_qr, s_qi = tiny(8), tiny(8)
        dxb, dtm, dte, dts, da, eacs, dec = [tiny(24) for _ in range(7)]
        aneg = tiny(12)
        acs = tiny(48)
        ssn, srs, srstd = tiny(2), tiny(2), tiny(2)
        mx = tiny(2 * 16)
        nb = tiny(2 * 16)
        den = tiny(2 * 16)
        dsk = tiny(2 * 16)
        qss = tiny(40)
        r_fac, r_fin = tiny(16), tiny(16)
        r_mid = tiny(16)
        r_bon = tiny(32)
        ka_h, ka_1 = tiny(8), tiny(8)
        gn_s, gn_m, gn_q = tiny(32), tiny(32), tiny(32)

        def w(name, i=0):
            return ring[:, (FIRST_CHUNK[name] + i) % RING, :]

        block = ctx.enter_context(nc.Block())

        @block.sync
        def _(sync):
            sync.wait_ge(in_x, 16)
            for n in range(N_CHUNKS):
                if n >= RING:
                    before = n - RING
                    if CHUNK_LAST[before] is not None:
                        sync.wait_ge(psum_full, CHUNK_LAST[before] + 1)
                    else:
                        i, k = [(i, before - FIRST_CHUNK[f"down{i}"]) for i in range(3)
                                if 0 <= before - FIRST_CHUNK[f"down{i}"] < 5][0]
                        sync.wait_ge(down_chunk_used, 5 * i + k + 1)
                sync.dma_start(ring[:, n % RING, :], io["wall"][n, :, :]).then_inc(chunk_in[n % RING], 16)

        @block.scalar
        def _(act):
            steps = [0]

            def step(instruction):
                steps[0] += 1
                instruction.then_inc(act_step, 1)

            def settle():
                act.wait_ge(act_step, steps[0])

            A = nc.scalar.activation
            for loaded, dst, src in ((in_x, x, io["x_tok"].rearrange("p (t d) -> p t d", t=TT)),
                                     (in_prm, prm[:, :], io["prm"]), (in_cst, cst[:, :], io["cst"]),
                                     (in_mem, memraw, io["mem_tok"].rearrange("p (t d) -> p t d", t=TT)),
                                     (in_rows, rows[:, :], io["rows"].to_broadcast([P, N_ROWS])),
                                     (in_s5b, s5b, io["s5b"]), (in_s5c, s5c, io["s5c"])):
                act.dma_start(dst, src).then_inc(loaded, 16)

            def squares(k, src, junk, ready):
                for tt in range(TT):
                    ready(tt)
                    n = 2 * k + tt
                    if tt and junk[0] is junk[1]:
                        act.wait_ge(sumsq, SUMSQ_AT[k])
                    A(junk[tt], src[:, tt, :], ACT.Square, accum_out=ss[:, n:n + 1]).then_inc(sumsq, 1)

            def sums_of_x(base):
                def ready(tt):
                    act.wait_ge(*when_read(base + tt))
                    act.wait_ge(*when_read(base + TT + tt))
                return ready

            xn_junk = [xn[:, tt, :] for tt in range(TT)]
            squares(0, x, xn_junk, lambda tt: act.wait_ge(in_x, 16))
            squares(1, memraw, [mem_junk] * TT, lambda tt: act.wait_ge(in_mem, 16))

            act.wait_ge(in_prm, 16)
            A(s_dt, col("log_dt", 0, 8), ACT.Exp).then_inc(s5_dt, 1)
            act.wait_ge(s5_lrdt, 1)
            A(s_mag, s_lrdt, ACT.Exp).then_inc(s5_mag, 1)
            act.wait_ge(s5_angle, 1)
            A(s_sin, s_r, ACT.Sin)
            A(s_cos, s_abs, ACT.Sin).then_inc(s5_trig, 1)
            act.wait_ge(psum_full, G["tx_mix"] + 3 + 1)
            act.dma_start(glu, io["glu"]).then_inc(in_glu, 16)

            def silu_tanh(i):
                act.wait_ge(*when_read(G["xbc"] + i))
                if i >= 2:
                    act.wait_ge(xc_ready, i - 1)
                A(thA[:, (i % 2) * 512:(i % 2) * 512 + 512], xc[:, 2 * i:2 * i + 2, :], ACT.Tanh).then_inc(xc_tanh, 1)

            act.wait_ge(halved, 1)
            for i in range(7):
                act.wait_ge(psum_full, G["xbc"] + i + 1)
                for j in range(2):
                    fb = 2 * i + j
                    ins = A(xc[:, fb, :], b_(G["xbc"] + i)[:, j * T:(j + 1) * T], ACT.Identity,
                            scale=col("conv_w", 3 * CONVB + fb), bias=col("conv_b", fb))
                ins.then_inc(xc_tap, 1)
                if i >= 1:
                    silu_tanh(i - 1)
            silu_tanh(6)
            act.wait_ge(psum_full, G["u"] + 1)
            A(uT, b_(G["u"]), ACT.Copy).then_inc(bank_sem(G["u"]), 1)
            for i in range(4):
                n = G["z"] + i
                width = 256 if i < 2 else 512
                act.wait_ge(psum_full, n + 1)
                act.wait_ge(xc_ready, 7)
                if i >= 2:
                    act.wait_ge(*when_read(n - 2))
                A(thA[:, (i % 2) * 512:(i % 2) * 512 + width], b_(n, width), ACT.Tanh, scale=0.5).then_inc(z_tanh, 1)
            act.wait_ge(dt_neg, 1)
            step(A(dte, dte, ACT.Exp))
            settle()
            step(A(dts, dte, ACT.Ln, bias=1.0))
            act.wait_ge(in_rows, 16)
            A(aneg, row("a_log", HEADS), ACT.Exp).then_inc(dt_ln, 1)
            for i in range(4):
                n = G["xa_k"] + i
                act.wait_ge(psum_full, n + 1)
                A(kT[:, 2 * i:2 * i + 2, :], b3(n, 2, T), ACT.Copy).then_inc(bank_sem(n), 1)
            for i in range(4):
                n = G["xa_v"] + i
                act.wait_ge(psum_full, n + 1)
                c, tt = i // 2, i % 2
                A(v_xa[:, tt, c * 512:c * 512 + 512], b_(n), ACT.Copy).then_inc(bank_sem(n), 1)
            for i in range(2):
                act.wait_ge(psum_full, G["cb"] + i + 1)
                A(cb[:, i * 512:i * 512 + 512], b_(G["cb"] + i), ACT.Copy).then_inc(bank_sem(G["cb"] + i), 1)
            for q in range(3):
                n = G["x_tok"] + q
                act.wait_ge(psum_full, n + 1)
                out = xtok[:, :, 256 * q:256 * q + 256].rearrange("p t (f c) -> p f t c", f=2)
                A(out, b_(n).rearrange("p (f t c) -> p f t c", f=2, t=TT), ACT.Copy).then_inc(bank_sem(n), 1)
            act.wait_ge(psum_full, G["b_tok"] + 1)
            A(btok, b_(G["b_tok"]), ACT.Copy).then_inc(bank_sem(G["b_tok"]), 1)
            act.wait_ge(acs_sub, 1)
            A(eacs, acs[:, 0:24], ACT.Exp)
            A(dec, dec, ACT.Exp).then_inc(decays, 1)
            for q in range(2):
                n = G["state"] + q
                act.wait_ge(psum_full, n + 1)
                A(prevT[:, 384 * q:384 * q + 384], b_(n, 384), ACT.Copy).then_inc(bank_sem(n), 1)
            act.wait_ge(s5_gelu_in, 1)
            A(y5g[:, 512:1024], y5g[:, 512:1024], ACT.Tanh, scale=math.sqrt(2 / math.pi)).then_inc(s5_gelu_tanh, 1)
            act.wait_ge(psum_full, G["s5_glu"] + 1)
            A(y5g[:, 512:1024], b_(G["s5_glu"]), ACT.Tanh, scale=0.5).then_inc(bank_sem(G["s5_glu"]), 1)
            for tt in range(TT):
                for g in range(GROUPS):
                    act.wait_ge(*when_read(G[f"row{tt}"] + g))
                    A(Lc[:, g * 384:g * 384 + 384], Lc[:, g * 384:g * 384 + 384], ACT.Exp).then_inc(lc_exp, 1)
            for tt in range(TT):
                act.wait_ge(y_gated, tt + 1)
                if tt:
                    act.wait_ge(ssd_sumsq, tt)
                A(triD[:, 0:768], y_t[:, tt, :], ACT.Square, accum_out=ssn[:, tt:tt + 1]).then_inc(ssd_sumsq, 1)
            squares(2, x, xn_junk, sums_of_x(G["w_out"]))
            for i in range(4):
                n = G["xa_q"] + i
                act.wait_ge(psum_full, n + 1)
                A(qT[:, 2 * i:2 * i + 2, :], b3(n, 2, T), ACT.Copy).then_inc(bank_sem(n), 1)
            for h in range(XA_H):
                n = G[f"xa_s{h}"]
                act.wait_ge(xa_max, h + 1)
                for tt in range(TT):
                    at = 2 * h + tt
                    ins = A(p_xa[:, at * 256:at * 256 + 256], b_(n)[:, tt * 256:tt * 256 + 256], ACT.Exp,
                            scale=1 / 16, bias=nb[:, at:at + 1], accum_out=den[:, at:at + 1])
                ins.then_inc(bank_sem(n), 1)
            for h in range(XA_H):
                n = G[f"xa_t{h}"]
                act.wait_ge(psum_full, n + 1)
                A(pT_xa[:, (h % 2) * 512:(h % 2) * 512 + 512], b_(n), ACT.Copy).then_inc(bank_sem(n), 1)
                n = G[f"xa_ov{h}"]
                act.wait_ge(psum_full, n + 1)
                A(oT[:, 2 * h:2 * h + 2, :], b3(n, 2, T), ACT.Copy).then_inc(bank_sem(n), 1)
            squares(3, x, xn_junk, sums_of_x(G["xa_o"]))
            act.wait_ge(psum_full, G["tx_ffn0"] + 3 + 1)
            act.dma_start(fnw, io["wide"][0:1, :].to_broadcast([P, D])).then_inc(in_fnw, 16)
            act.dma_start(swc, io["swc"]).then_inc(in_swc, 16)

            def ffn(i, value_conv):
                for c in range(11):
                    n = G[f"up{i}"] + 2 * c
                    at = 11 * i + c
                    tap = 2 if i == 0 else 1
                    nb_ = FB if i == 0 else 2 * FB
                    act.wait_ge(psum_full, n + 1)
                    if c >= 2:
                        act.wait_ge(act_ready, at - 1)
                    for j in range(2):
                        fb = 2 * c + j
                        ins = A(f_acc[:, (c % 2) * 512 + j * T:][:, :T], b_(n)[:, j * T:(j + 1) * T], ACT.Identity,
                                scale=col(f"fcw{i}", tap * nb_ + fb), bias=col(f"fcb{i}", fb))
                    ins.then_inc(gate_tap, 1)
                    if value_conv:
                        act.wait_ge(psum_full, n + 1 + 1)
                        for j in range(2):
                            fb = FB + 2 * c + j
                            ins = A(f_val[:, (c % 2) * 512 + j * T:][:, :T], b_(n + 1)[:, j * T:(j + 1) * T],
                                    ACT.Identity, scale=col(f"fcw{i}", tap * nb_ + fb), bias=col(f"fcb{i}", fb))
                        ins.then_inc(value_tap, 1)
                    act.wait_ge(*when_read(n))
                    A(f_th[:, (c % 2) * 512:][:, :512], f_acc[:, (c % 2) * 512:][:, :512], ACT.Tanh).then_inc(gate_tanh, 1)

            ffn(0, False)
            squares(4, x, xn_junk, sums_of_x(G["down0"]))
            for tt in range(TT):
                act.wait_ge(x_final_norm, tt + 1)
                n = 2 * 5 + tt
                A(xn[:, tt, :], x[:, tt, :], ACT.Square, accum_out=ss[:, n:n + 1]).then_inc(sumsq, 1)
            for c in range(3):
                for tt in range(TT):
                    n = G["qkv"] + 2 * c + tt
                    act.wait_ge(psum_full, n + 1)
                    A(qkv[:, tt, c * 512:c * 512 + 512], b_(n), ACT.Copy).then_inc(bank_sem(n), 1)
            for tt in range(TT):
                for c in range(3):
                    act.wait_ge(*when_read(G["qkv"] + 2 * c + tt))
                if tt:
                    act.wait_ge(qk_sums, tt)
                A(w_sq, qkv[:, tt, 0:1280], ACT.Square).then_inc(qk_square, 1)
            for q in range(4):
                n = G["q_tr"] + q
                act.wait_ge(psum_full, n + 1)
                A(w_qT[:, 2 * q:2 * q + 2, :], b3(n, 2, T), ACT.Copy).then_inc(bank_sem(n), 1)
            act.wait_ge(psum_full, G["k_tr"] + 1)
            A(w_kT, b3(G["k_tr"], 2, T), ACT.Copy).then_inc(bank_sem(G["k_tr"]), 1)

            def window_exp(q):
                for i in range(4):
                    h = 4 * q + i
                    act.wait_ge(sw_max, h + 1)
                    for tt in range(TT):
                        at = 2 * h + tt
                        ins = A(w_p[:, (h % 8) * 512 + tt * T:][:, :T], w_p[:, (h % 8) * 512 + tt * T:][:, :T], ACT.Exp,
                                scale=1 / 8, bias=nb[:, at:at + 1], accum_out=den[:, at:at + 1])
                    A(dsk[:, 2 * h:2 * h + 2], nb[:, 2 * h:2 * h + 2], ACT.Exp, bias=row("sinks", 1, h)).then_inc(sw_exp, 1)

            def window_out(q):
                for i in range(4):
                    h = 4 * q + i
                    n = G[f"sw_t{q}"] + i
                    act.wait_ge(psum_full, n + 1)
                    A(w_pT[:, (h % 4) * 512:][:, :512], b_(n), ACT.Copy).then_inc(bank_sem(n), 1)
                n = G[f"sw_ov{q}"]
                act.wait_ge(psum_full, n + 1)
                A(w_oT[:, 2 * q:2 * q + 2, :], b3(n, 2, T), ACT.Copy).then_inc(bank_sem(n), 1)

            window_exp(0)
            for q in range(4):
                if q < 3:
                    window_exp(q + 1)
                window_out(q)
            squares(6, x, xn_junk, sums_of_x(G["swa_o"]))
            ffn(1, True)
            squares(7, x, xn_junk, sums_of_x(G["down1"]))
            act.dma_start(back, io["back"]).then_inc(in_back, 16)
            act.dma_start(masks_in, io["masks"]).then_inc(in_masks, 16)
            for i in range(4):
                n = G["rw_r"] + i
                act.wait_ge(psum_full, n + 1)
                A(r_rT3[:, 2 * i:2 * i + 2, :], b3(n, 2, T), ACT.Copy).then_inc(bank_sem(n), 1)
            for i in range(4):
                n = G["rw_k"] + i
                act.wait_ge(psum_full, n + 1)
                A(r_kT3[:, 2 * i:2 * i + 2, :], b3(n, 2, T), ACT.Copy).then_inc(rw_k_copied, 1)
                act.wait_ge(*when_read(n))
                act.wait_ge(masks_made, 1)
                A(r_LA[:, 512 * i:512 * i + 512].rearrange("p (k t) -> p k t", k=2),
                       r_kk3[:, 2 * i:2 * i + 2, :], ACT.Square).then_inc(kk_square, 1)
            for i in range(4):
                n = G["rw_v"] + i
                act.wait_ge(psum_full, n + 1)
                c, tt = i // 2, i % 2
                A(r_vt[:, tt, c * 512:c * 512 + 512], b_(n), ACT.Copy).then_inc(bank_sem(n), 1)
            n = G["lora1"]
            act.wait_ge(psum_full, n + 1)
            A(r_low[:, 0:T], b_(n)[:, 0:T], ACT.Tanh)
            A(r_low[:, T:2 * T], b_(n)[:, T:2 * T], ACT.Copy).then_inc(bank_sem(n), 1)
            n += 1
            act.wait_ge(psum_full, n + 1)
            step(A(r_sg[:, 0:T], b_(n)[:, 0:T], ACT.Tanh, scale=0.5))
            A(r_sg[0:32, T:2 * T], b_(n)[0:32, T:2 * T], ACT.Tanh, scale=0.5).then_inc(bank_sem(n), 1)

            def decay_tanh(d, i):
                n = G[f"wl{d}_{i}"]
                act.wait_ge(psum_full, n + 1)
                for j in range(2):
                    fb = 2 * i + j
                    ins = A(hflat[:, fb * T:(fb + 1) * T], b_(n)[:, j * T:(j + 1) * T], ACT.Tanh,
                            scale=0.5, bias=col("w0", 8 * d + fb))
                ins.then_inc(bank_sem(n), 1)

            def rw_direction(d):
                if d == 0:
                    for i in range(4):
                        decay_tanh(0, i)
                act.wait_ge(cum_done, d + 1)
                for i in range(4):
                    n = G[f"al{d}"] + i
                    act.wait_ge(psum_full, n + 1)
                    for j in range(2):
                        fb = 2 * i + j
                        ins = A(r_LA[:, fb * T:(fb + 1) * T], b_(n)[:, j * T:(j + 1) * T], ACT.Tanh,
                                scale=0.5, bias=col("a0", 8 * d + fb))
                    ins.then_inc(bank_sem(n), 1)
                A(r_TT, xn_flat[:, :], ACT.Exp, scale=0.5 * DECAY).then_inc(e_up, 1)
                A(xn_flat[:, :], xn_flat[:, :], ACT.Exp, scale=-0.5 * DECAY).then_inc(e_down, 1)
                A(hflat, hflat, ACT.Exp, scale=-0.5 * DECAY).then_inc(e_before, 1)
                A(r_fac[:, 8 * d:8 * d + 8], r_fin[:, 8 * d:8 * d + 8], ACT.Exp, scale=-0.5 * DECAY).then_inc(e_state, 1)
                for q in range(4):
                    n = G[f"bk_tok{d}"] + q
                    act.wait_ge(psum_full, n + 1)
                    out = r_bk.rearrange("p (a k c) -> p a k c", a=2, k=KB)[:, :, 2 * q:2 * q + 2, :]
                    A(out, b_(n).rearrange("p (a k c) -> p a k c", a=2, k=2), ACT.Copy).then_inc(bank_sem(n), 1)
                for order in (0, 1):
                    for half in (0, 1):
                        b = f"{d}{order}{half}"
                        for lv in range(1, LEVELS):
                            for g2 in range(2):
                                product, transposed, _ = level_groups(lv, b, g2)
                                if lv == 1:
                                    act.wait_ge(psum_full, transposed + 1)
                                    A(r_Tk[:, 4 * g2:4 * g2 + 4, 0], b3(transposed, 4, P), ACT.Copy).then_inc(bank_sem(transposed), 1)
                                    continue
                                act.wait_ge(psum_full, product + 1)
                                A(r_Yb[:, 512 * g2:512 * g2 + 512], b_(product), ACT.Copy).then_inc(bank_sem(product), 1)
                                act.wait_ge(psum_full, transposed + 1)
                                A(r_Tk[:, 4 * g2:4 * g2 + 4, 1], b3(transposed, 4, P), ACT.Copy).then_inc(bank_sem(transposed), 1)
                            if lv == 1:
                                for g2 in range(2):
                                    product = level_groups(lv, b, g2)[0]
                                    act.wait_ge(psum_full, product + 1)
                                    A(r_Yb[:, 512 * g2:512 * g2 + 512], b_(product), ACT.Copy).then_inc(bank_sem(product), 1)
                            if b == "011" and lv <= 4:
                                decay_tanh(1, lv - 1)
                        n = G["xs" + b]
                        act.wait_ge(psum_full, n + 1)
                        A(r_X, b_(n), ACT.Copy).then_inc(bank_sem(n), 1)
                        n = G["us" + b]
                        act.wait_ge(psum_full, n + 1)
                        A(r_U, b_(n), ACT.Copy).then_inc(bank_sem(n), 1)

            for d in range(2):
                rw_direction(d)
            act.wait_ge(psum_full, G["ys111"] + 1)
            act.dma_start(lnx[:, 0:D], io["wide"][1:2, :].to_broadcast([P, D])).then_inc(in_lnx, 16)
            act.dma_start(lnx[:, D:2 * D], io["wide"][2:3, :].to_broadcast([P, D])).then_inc(in_lnx, 16)
            act.wait_ge(y_centred, 1)
            A(r_AR[:, 0:2048], r_y, ACT.Square).then_inc(gn_square, 1)
            for q in range(4):
                n = G["tx_y"] + q
                act.wait_ge(psum_full, n + 1)
                A(r_oT[:, 2 * q:2 * q + 2, :], b3(n, 2, T), ACT.Copy).then_inc(bank_sem(n), 1)
            squares(8, x, xn_junk, sums_of_x(G["rw_o"]))
            ffn(2, True)
            for c in range(2):
                for tt in range(TT):
                    act.wait_ge(*when_read(G["down2"] + 2 * c + tt))
            act.dma_start(io["y"].rearrange("(t p) d -> p t d", p=P), x).then_inc(out_done, 16)
            act.wait_ge(out_done, 16)

        @block.tensor
        def _(pe):
            mm = nc.tensor.matmul

            def chunk(name, i=0):
                n = FIRST_CHUNK[name] + i
                pe.wait_ge(chunk_in[n % RING], 16 * (n // RING + 1))
                return w(name, i)

            def transposes(n, blocks):
                if n >= BANKS:
                    pe.wait_ge(*when_read(n - BANKS))
                for j, src in enumerate(blocks):
                    ins = nc.tensor.transpose(b_(n)[:, j * P:(j + 1) * P], src, ident)
                ins.then_inc(psum_full, 1)

            def norm_transposes(k, n, src):
                for tt in range(TT):
                    pe.wait_ge(normed, NORM_AT[k] + tt)
                    for q in range(2):
                        transposes(n + 2 * tt + q, [src[:, tt, (4 * q + j) * P:][:, :P] for j in range(4)])

            def features(n, wc, cols, xT, blocks=KB):
                if n >= BANKS:
                    pe.wait_ge(*when_read(n - BANKS))
                for j, c0 in enumerate(cols):
                    for kb in range(blocks):
                        ins = mm(b_(n)[:, j * T:(j + 1) * T], lhsT=wc[:, kb * 512 + c0:][:, :P], rhs=xT[:, kb, :],
                                 start=kb == 0, stop=kb == blocks - 1)
                ins.then_inc(psum_full, 1)

            def tokens(n, wc, c0, width, xT, tt):
                if n >= BANKS:
                    pe.wait_ge(*when_read(n - BANKS))
                for kb in range(KB):
                    ins = mm(b_(n, width), lhsT=xT[:, kb, tt * P:(tt + 1) * P], rhs=wc[:, kb * 512 + c0:][:, :width],
                             start=kb == 0, stop=kb == KB - 1)
                ins.then_inc(psum_full, 1)

            def square_features(name, xT):
                for c in range(2):
                    wc = chunk(name, c)
                    for i in range(2):
                        features(G[name] + 2 * c + i, wc, (256 * i, 256 * i + P), xT)

            def square_tokens(name, xT):
                for c in range(2):
                    wc = chunk(name, c)
                    for tt in range(TT):
                        tokens(G[name] + 2 * c + tt, wc, 0, 512, xT, tt)

            def normed_in(name):
                for i in range(4):
                    pe.wait_ge(*when_read(G[name] + i))

            pe.wait_ge(in_cst, 16)
            norm_transposes(0, G["tx_mix"], xn)
            norm_transposes(1, G["tx_mem"], memraw)
            normed_in("tx_mix")
            for i in range(7):
                features(G["xbc"] + i, chunk("w_in", i // 2), (256 * (i % 2), 256 * (i % 2) + P), h_mid)
            if G["dt"] >= BANKS:
                pe.wait_ge(*when_read(G["dt"] - BANKS))
            wc = chunk("w_in", 3)
            for tt in range(TT):
                for kb in range(KB):
                    ins = mm(b_(G["dt"])[:, tt * HEADS:(tt + 1) * HEADS], lhsT=h_mid[:, kb, tt * P:(tt + 1) * P],
                             rhs=wc[:, kb * 512 + 256:][:, :HEADS], start=kb == 0, stop=kb == KB - 1)
            ins.then_inc(psum_full, 1)
            wc = chunk("w_in", 4)
            features(G["u"], wc, (0, P), h_mid)
            for tt in range(TT):
                tokens(G["z"] + tt, wc, 256, 256, h_mid, tt)
            wc = chunk("w_in", 5)
            for tt in range(TT):
                tokens(G["z"] + 2 + tt, wc, 0, 512, h_mid, tt)
            pe.wait_ge(*when_read(G["u"]))
            pe.wait_ge(in_s5b, 16)
            for j in range(S5_TILES):
                n = G["s5_bu"] + j
                if n >= BANKS:
                    pe.wait_ge(*when_read(n - BANKS))
                rows_ = slice(32 * (j % 4), 32 * (j % 4) + 32)
                for r in range(2):
                    ins = mm(b_(n)[:, r * T:(r + 1) * T], lhsT=s5b[rows_, (2 * r + j // 4) * P:][:, :P],
                             rhs=uT3[rows_, j // 4, :], start=True, stop=True)
                ins.then_inc(psum_full, 1)
            normed_in("tx_mem")
            square_features("xa_k", memT)
            n = G["acs"]
            if n >= BANKS:
                pe.wait_ge(*when_read(n - BANKS))
            pe.wait_ge(da_ready, 1)
            mm(b_(n)[:, 0:24], lhsT=c_("tri", P), rhs=da, start=True, stop=True)
            mm(b_(n)[:, 24:48], lhsT=c_("ones", P), rhs=da, start=True, stop=True).then_inc(psum_full, 1)
            square_tokens("xa_v", memT)
            pe.wait_ge(xc_ready, 7)
            for tt in range(TT):
                n = G["cb"] + tt
                if n >= BANKS:
                    pe.wait_ge(*when_read(n - BANKS))
                for g in range(GROUPS):
                    ins = mm(b_(n)[:, g * P:(g + 1) * P], lhsT=xc[:, XB + g, tt * P:(tt + 1) * P],
                             rhs=xc[:, XB + GROUPS + g, tt * P:(tt + 1) * P], start=True, stop=True)
                ins.then_inc(psum_full, 1)
            for q in range(3):
                transposes(G["x_tok"] + q, [xc[:, 2 * q + f, tt * P:(tt + 1) * P] for f in range(2) for tt in range(TT)])
            transposes(G["b_tok"], [xc[:, XB + g, 0:P] for g in range(GROUPS)])
            pe.wait_ge(*when_read(G["b_tok"]))
            pe.wait_ge(xdt_ready, 1)
            for q in range(2):
                n = G["state"] + q
                if n >= BANKS:
                    pe.wait_ge(*when_read(n - BANKS))
                for i in range(2):
                    g = 2 * q + i
                    ins = mm(b_(n)[:, i * 192:(i + 1) * 192], lhsT=btok[:, g * P:(g + 1) * P],
                             rhs=xdtd[:, g * 192:(g + 1) * 192], start=True, stop=True)
                ins.then_inc(psum_full, 1)
            n = G["s5_y"]
            if n >= BANKS:
                pe.wait_ge(*when_read(n - BANKS))
            pe.wait_ge(s5_cw, 1)
            for j in range(S5_TILES):
                pe.wait_ge(s5_h, j + 1)
                for r in range(2):
                    ins = mm(b_(n)[32 * (j % 4):32 * (j % 4) + 32, (j // 4) * T:][:, :T],
                             lhsT=cw[:, 256 * r + 32 * j:][:, :32], rhs=(Er, Ei)[r][:, j, :],
                             start=r == 0, stop=r == 1, tile_position=(0, 32 * (j % 4)))
            ins.then_inc(psum_full, 1)
            n = G["s5_glu"]
            if n >= BANKS:
                pe.wait_ge(*when_read(n - BANKS))
            pe.wait_ge(s5_gelu, 1)
            pe.wait_ge(in_glu, 16)
            for j in range(2):
                for kb in range(2):
                    ins = mm(b_(n)[:, j * T:(j + 1) * T], lhsT=glu[:, kb * S5_W + j * P:][:, :P],
                             rhs=y5g[:, kb * T:(kb + 1) * T], start=kb == 0, stop=kb == 1)
            ins.then_inc(psum_full, 1)
            for tt in range(TT):
                for g in range(GROUPS):
                    n = G[f"row{tt}"] + g
                    if n >= BANKS:
                        pe.wait_ge(*when_read(n - BANKS))
                    pe.wait_ge(trid_ready, GROUPS * tt + g + 1)
                    mm(b_(n, 384), lhsT=c_("ones", P), rhs=triD[:, (g % 2) * 384:][:, :384], start=True, stop=True).then_inc(psum_full, 1)
                for q in range(2):
                    n = G[f"diag{tt}"] + q
                    if n >= BANKS:
                        pe.wait_ge(*when_read(n - BANKS))
                    pe.wait_ge(lc_ready, GROUPS * tt + 2 * q + 2)
                    for i in range(6):
                        hh = 6 * q + i
                        ins = mm(b_(n)[:, i * HD:(i + 1) * HD], lhsT=Lc[:, hh * P:(hh + 1) * P],
                                 rhs=xdt_t[:, tt, hh * HD:(hh + 1) * HD], start=True, stop=True)
                    ins.then_inc(psum_full, 1)
            for q in range(2):
                n = G["off"] + q
                if n >= BANKS:
                    pe.wait_ge(*when_read(n - BANKS))
                pe.wait_ge(*when_read(G["state"] + q))
                for i in range(2):
                    g = 2 * q + i
                    ins = mm(b_(n)[:, i * 192:(i + 1) * 192], lhsT=xc[:, XB + GROUPS + g, P:2 * P],
                             rhs=prevT[:, g * 192:(g + 1) * 192], start=True, stop=True)
                ins.then_inc(psum_full, 1)
            pe.wait_ge(y_normed, 2)
            for q in range(3):
                transposes(G["tx_ssd"] + q, [y_t[:, tt, (2 * q + f) * P:][:, :P] for f in range(2) for tt in range(TT)])
            pe.wait_ge(s5_done, 1)
            for q in range(3):
                pe.wait_ge(*when_read(G["tx_ssd"] + q))
            for c in range(2):
                wc = chunk("w_out", c)
                for tt in range(TT):
                    n = G["w_out"] + 2 * c + tt
                    if n >= BANKS:
                        pe.wait_ge(*when_read(n - BANKS))
                    for kb in range(KB):
                        src = y5T3[:, kb] if kb < 2 else yT[:, kb - 2]
                        ins = mm(b_(n), lhsT=src[:, tt * P:(tt + 1) * P], rhs=wc[:, kb * 512:(kb + 1) * 512],
                                 start=kb == 0, stop=kb == KB - 1)
                    ins.then_inc(psum_full, 1)
            norm_transposes(2, G["tx_xa"], xn)
            normed_in("tx_xa")
            square_features("xa_q", h_mid)
            for h in range(XA_H):
                n = G[f"xa_s{h}"]
                if n >= BANKS:
                    pe.wait_ge(*when_read(n - BANKS))
                pe.wait_ge(*when_read(G["xa_q"] + h))
                pe.wait_ge(*when_read(G["xa_k"] + h))
                for tt in range(TT):
                    for db in range(2):
                        ins = mm(b_(n)[:, tt * T:(tt + 1) * T], lhsT=qT[:, 2 * h + db, tt * P:(tt + 1) * P],
                                 rhs=kT[:, 2 * h + db, :], start=db == 0, stop=db == 1)
                ins.then_inc(psum_full, 1)
            for h in range(XA_H):
                pe.wait_ge(xa_p, h + 1)
                p = p_xa[:, h * 512:(h + 1) * 512]
                transposes(G[f"xa_t{h}"], [p[:, tt * T + m * P:][:, :P] for m in range(TT) for tt in range(TT)])
                n = G[f"xa_ov{h}"]
                if n >= BANKS:
                    pe.wait_ge(*when_read(n - BANKS))
                pe.wait_ge(*when_read(G[f"xa_t{h}"]))
                for i in range(4):
                    pe.wait_ge(*when_read(G["xa_v"] + i))
                for db in range(2):
                    for m in range(TT):
                        ins = mm(b_(n)[:, db * T:(db + 1) * T], lhsT=v_xa[:, m, h * 256 + db * P:][:, :P],
                                 rhs=pT_xa[:, (h % 2) * 512 + m * T:][:, :T], start=m == 0, stop=m == TT - 1)
                ins.then_inc(psum_full, 1)
            for h in range(XA_H):
                pe.wait_ge(*when_read(G[f"xa_ov{h}"]))
            square_tokens("xa_o", oT)

            def ffn(i, k):
                norm_transposes(k, G[f"tx_ffn{i}"], xn)
                normed_in(f"tx_ffn{i}")
                for c in range(11):
                    wc = chunk(f"up{i}", c)
                    for j in range(2):
                        features(G[f"up{i}"] + 2 * c + j, wc, (256 * j, 256 * j + P), h_mid)
                base = G[f"down{i}"]
                for r in range(4):
                    if base + r >= BANKS:
                        pe.wait_ge(*when_read(base + r - BANKS))
                for fb in range(FB):
                    wc = chunk(f"down{i}", fb // 4)
                    pe.wait_ge(act_ready, 11 * i + fb // 2 + 1)
                    for c in range(2):
                        for tt in range(TT):
                            ins = mm(b_(base + 2 * c + tt), lhsT=actT[:, fb, tt * P:(tt + 1) * P],
                                     rhs=wc[:, (fb % 4) * D + c * 512:][:, :512], start=fb == 0, stop=fb == FB - 1)
                            if fb == FB - 1:
                                ins.then_inc(psum_full, 1)
                    if fb % 4 == 3:
                        ins.then_inc(down_chunk_used, 1)

            ffn(0, 3)
            norm_transposes(5, G["tx_swa"], xn)
            normed_in("tx_swa")
            for c in range(3):
                wc = chunk("qkv", c)
                for tt in range(TT):
                    tokens(G["qkv"] + 2 * c + tt, wc, 0, 512, h_mid, tt)
            pe.wait_ge(roped, 2)
            for q in range(4):
                transposes(G["q_tr"] + q, [qkv[:, tt, (2 * q + f) * P:][:, :P] for f in range(2) for tt in range(TT)])
            transposes(G["k_tr"], [qkv[:, tt, D + f * P:][:, :P] for f in range(2) for tt in range(TT)])
            pe.wait_ge(*when_read(G["k_tr"]))

            def window_scores(q):
                for i in range(4):
                    h = 4 * q + i
                    at = slice(HD * (h % 2), HD * (h % 2) + HD)
                    n = G[f"sw_s{q}"] + i
                    if n >= BANKS:
                        pe.wait_ge(*when_read(n - BANKS))
                    pe.wait_ge(*when_read(G["q_tr"] + h // 4))
                    for tt in range(TT):
                        ins = mm(b_(n)[:, tt * T:(tt + 1) * T], lhsT=w_qT[at, h // 2, tt * P:(tt + 1) * P],
                                 rhs=w_kT[at, h // 8, :], start=True, stop=True)
                    ins.then_inc(psum_full, 1)

            def window_values(q):
                for i in range(4):
                    h = 4 * q + i
                    pe.wait_ge(sw_p, h + 1)
                    p = w_p[:, (h % 8) * 512:][:, :512]
                    transposes(G[f"sw_t{q}"] + i, [p[:, tt * T + m * P:][:, :P] for m in range(TT) for tt in range(TT)])
                n = G[f"sw_ov{q}"]
                if n >= BANKS:
                    pe.wait_ge(*when_read(n - BANKS))
                for i in range(4):
                    h = 4 * q + i
                    kv = 2 * (h // 8) + h % 2
                    pe.wait_ge(*when_read(G[f"sw_t{q}"] + i))
                    for m in range(TT):
                        ins = mm(b_(n)[HD * (h % 2):HD * (h % 2) + HD, (i // 2) * T:][:, :T],
                                 lhsT=qkv[:, m, 1280 + kv * HD:][:, :HD], rhs=w_pT[:, (h % 4) * 512 + m * T:][:, :T],
                                 start=m == 0, stop=m == TT - 1, tile_position=(0, HD * (h % 2)))
                ins.then_inc(psum_full, 1)

            window_scores(0)
            for q in range(4):
                if q < 3:
                    window_scores(q + 1)
                window_values(q)
            for q in range(4):
                pe.wait_ge(*when_read(G[f"sw_ov{q}"]))
            square_tokens("swa_o", w_oT)
            ffn(1, 6)
            norm_transposes(7, G["tx_rw"], xn)
            pe.wait_ge(x_mixed, 1)
            square_features("rw_r", x_mix[0])
            pe.wait_ge(x_mixed, 2)
            square_features("rw_k", x_mix[1])
            pe.wait_ge(x_mixed, 3)
            square_tokens("rw_v", x_mix[0])
            n = G["kk_ss"]
            if n >= BANKS:
                pe.wait_ge(*when_read(n - BANKS))
            for i in range(4):
                pe.wait_ge(kk_square, i + 1)
            for fb in range(KB):
                ins = mm(b_(n)[0:16, 0:T], lhsT=c_("headsel", KB * 16)[:, 16 * fb:16 * fb + 16],
                         rhs=r_LA[:, fb * T:(fb + 1) * T], start=fb == 0, stop=fb == KB - 1)
            ins.then_inc(psum_full, 1)
            wc = chunk("lora1")
            if G["lora1"] >= BANKS:
                pe.wait_ge(*when_read(G["lora1"] - BANKS))
            for i in range(2):
                pe.wait_ge(x_mixed, 4 + i)
                for kb in range(KB):
                    ins = mm(b_(G["lora1"])[:, i * T:(i + 1) * T], lhsT=wc[:, kb * 512 + i * P:][:, :P],
                             rhs=x_mix[1 - i][:, kb, :], start=kb == 0, stop=kb == KB - 1)
            ins.then_inc(psum_full, 1)
            pe.wait_ge(x_mixed, 6)
            n = G["lora1"] + 1
            if n >= BANKS:
                pe.wait_ge(*when_read(n - BANKS))
            for i, m in enumerate((P, 32)):
                for kb in range(KB):
                    ins = mm(b_(n)[0:m, i * T:(i + 1) * T], lhsT=wc[:, kb * 512 + 256 + i * P:][:, :m],
                             rhs=x_mix[1][:, kb, :], start=kb == 0, stop=kb == KB - 1)
            ins.then_inc(psum_full, 1)
            pe.wait_ge(kk_rnorm, 1)
            pe.wait_ge(in_back, 16)
            for q in range(4):
                n = G["kk_bc"] + q
                if n >= BANKS:
                    pe.wait_ge(*when_read(n - BANKS))
                for j in range(2):
                    ins = mm(b_(n)[:, j * T:(j + 1) * T], lhsT=back[:, (2 * q + j) * P:][:, :P],
                             rhs=r_X[0:16, 0:T], start=True, stop=True)
                ins.then_inc(psum_full, 1)
            wl = chunk("lora2")
            pe.wait_ge(*when_read(G["lora1"]))

            def low_rank(name, d, q):
                n = G[f"wl{d}_{q}"] if name == "wl" else G[f"al{d}"] + q
                at, x0 = (0, 0) if name == "wl" else (D, T)
                if n >= BANKS:
                    pe.wait_ge(*when_read(n - BANKS))
                for j in range(2):
                    ins = mm(b_(n)[:, j * T:(j + 1) * T], lhsT=wl[HD * d:HD * d + HD, at + (2 * q + j) * P:][:, :P],
                             rhs=r_low[HD * d:HD * d + HD, x0:x0 + T], start=True, stop=True)
                ins.then_inc(psum_full, 1)

            def rw_direction(d):
                if d == 0:
                    for q in range(4):
                        low_rank("wl", 0, q)
                for q in range(4):
                    low_rank("al", d, q)
                n = G[f"bonus{d}"]
                if n >= BANKS:
                    pe.wait_ge(*when_read(n - BANKS))
                pe.wait_ge(rks_ready, d + 1)
                for tt in range(TT):
                    for fb in range(KB):
                        ins = mm(b_(n)[:, tt * 16:(tt + 1) * 16], lhsT=r_LA[:, fb * T + tt * P:][:, :P],
                                 rhs=c_("headsel", KB * 16)[:, 16 * fb:16 * fb + 16], start=fb == 0, stop=fb == KB - 1)
                ins.then_inc(psum_full, 1)
                pe.wait_ge(abkr_ready, d + 1)
                pe.wait_ge(b_scaled, d + 1)
                for q in range(4):
                    tile = slice(P * d, P * d + P)
                    transposes(G[f"bk_tok{d}"] + q, [src[:, 2 * q + j, tile] for src in (r_bh3, r_kh3) for j in range(2)])
                for j in range(8):
                    products(BATCHES[d][0], j)
                for at, b in enumerate(BATCHES[d]):
                    rw_batch(d, at // 2, at % 2, BATCHES[d][at + 1] if at < 3 else None)

            def products(b, j):
                d, order, half = map(int, b)
                tile = order if d == 0 else 1 - order
                src, pp, s = (r_bh3, r_kh3)[j // 4], j // 2 % 2, j % 2
                n = G[f"ab{b}_{j}"]
                if n >= BANKS:
                    pe.wait_ge(*when_read(n - BANKS))
                for i in range(2):
                    fb = 4 * half + 2 * pp + i
                    ins = mm(b_(n)[:, i * 256:(i + 1) * 256], lhsT=src[HD * s:HD * s + HD, fb, tile * P:(tile + 1) * P],
                             rhs=r_AR5[HD * s:HD * s + HD, fb, tile, :, :].rearrange("p a t -> p (a t)"),
                             start=True, stop=True)
                ins.then_inc(psum_full, 1)

            def rw_batch(d, order, half, following):
                b = f"{d}{order}{half}"
                tile = order if d == 0 else 1 - order
                units = [(pp, s) for pp in range(2) for s in range(2)]
                LA, LB = LAs[half], LBs[half]
                L = per_head(LA)
                for lv in range(1, LEVELS):
                    if lv == 1:
                        pe.wait_ge(t_start, BATCH_AT[d, order, half] + 1)
                        for g2 in range(2):
                            transposes(level_groups(lv, b, g2)[1], [r_Tk[:, 4 * g2 + k, 1] for k in range(4)])
                    for g2 in range(2):
                        product, transposed, _ = level_groups(lv, b, g2)
                        if lv == 1:
                            pe.wait_ge(*when_read(transposed))
                        else:
                            pe.wait_ge(*when_read(level_groups(lv - 1, b, g2)[2]))
                        if product >= BANKS:
                            pe.wait_ge(*when_read(product - BANKS))
                        for k in range(4):
                            ins = mm(b_(product)[:, k * P:(k + 1) * P], lhsT=L[:, 4 * g2 + k, 0],
                                     rhs=r_Tk[:, 4 * g2 + k, 0], start=True, stop=True)
                        ins.then_inc(psum_full, 1)
                        if lv > 1:
                            transposes(transposed, [r_Tk[:, 4 * g2 + k, 0] for k in range(4)])
                    for g2 in range(2):
                        product, transposed, update = level_groups(lv, b, g2)
                        if update >= BANKS:
                            pe.wait_ge(*when_read(update - BANKS))
                        pe.wait_ge(*when_read(product))
                        pe.wait_ge(*when_read(transposed))
                        for k in range(4):
                            Tt, Y = r_Tk[:, 4 * g2 + k, 1], r_Yb[:, (4 * g2 + k) * P:][:, :P]
                            first, second = (Tt, Y) if lv < LEVELS - 1 else (Y, Tt)
                            ins = mm(b_(update)[:, k * P:(k + 1) * P], lhsT=first, rhs=second, start=True, stop=True)
                        ins.then_inc(psum_full, 1)
                    if following and lv <= 4:
                        products(following, 2 * lv - 2)
                        products(following, 2 * lv - 1)
                    elif d == 0 and not following and lv <= 4:
                        low_rank("wl", 1, lv - 1)
                items = [(u, i, pp, s) for u, (pp, s) in enumerate(units) for i in range(2)]
                n = G["xs" + b]
                if n >= BANKS:
                    pe.wait_ge(*when_read(n - BANKS))
                if order:
                    pe.wait_ge(*when_read(G[f"ss{d}0{half}"]))
                for f4 in range(4):
                    fb = 4 * half + f4
                    if order:
                        mm(b_(n)[:, f4 * P:(f4 + 1) * P], lhsT=r_AR5[:, fb, tile, 0, :],
                           rhs=r_S[:, fb * P:(fb + 1) * P], start=True, stop=False)
                    for s in range(2):
                        u, i = 2 * (f4 // 2) + s, f4 % 2
                        pe.wait_ge(*when_read(G[f"ab{b}_{4 + u}"]))
                        ins = mm(b_(n)[:, (2 * f4 + s) * HD:][:, :HD], lhsT=LB[:, u * 512 + i * 256:][:, :P],
                                 rhs=r_vt[:, tile, (2 * fb + s) * HD:][:, :HD], start=order == 0, stop=order == 0 or s == 1)
                ins.then_inc(psum_full, 1)
                n = G["us" + b]
                if n >= BANKS:
                    pe.wait_ge(*when_read(n - BANKS))
                pe.wait_ge(*when_read(G["xs" + b]))
                for u, i, pp, s in items:
                    hl = 2 * (2 * pp + i) + s
                    pe.wait_ge(*when_read(level_groups(LEVELS - 1, b, u // 2)[2]))
                    ins = mm(b_(n)[:, hl * HD:(hl + 1) * HD], lhsT=r_TT[:, u * 512 + i * 256 + P:][:, :P],
                             rhs=r_X[:, hl * HD:(hl + 1) * HD], start=True, stop=True)
                ins.then_inc(psum_full, 1)
                n = G["ys" + b]
                if n >= BANKS:
                    pe.wait_ge(*when_read(n - BANKS))
                pe.wait_ge(*when_read(G["us" + b]))
                for f4 in range(4):
                    fb = 4 * half + f4
                    if order:
                        mm(b_(n)[:, f4 * P:(f4 + 1) * P], lhsT=r_AR5[:, fb, tile, 1, :],
                           rhs=r_S[:, fb * P:(fb + 1) * P], start=True, stop=False)
                    for s in range(2):
                        u, i, hl = 2 * (f4 // 2) + s, f4 % 2, 2 * f4 + s
                        out = b_(n)[:, hl * HD:(hl + 1) * HD]
                        mm(out, lhsT=LA[:, u * 512 + i * 256 + P:][:, :P], rhs=r_U[:, hl * HD:(hl + 1) * HD],
                           start=order == 0, stop=False)
                        ins = mm(out, lhsT=LB[:, u * 512 + i * 256 + P:][:, :P],
                                 rhs=r_vt[:, tile, (2 * fb + s) * HD:][:, :HD], start=False, stop=order == 0 or s == 1)
                ins.then_inc(psum_full, 1)
                if order == 0:
                    n = G["ss" + b]
                    if n >= BANKS:
                        pe.wait_ge(*when_read(n - BANKS))
                    for q in range(4):
                        pe.wait_ge(*when_read(G[f"bk_tok{d}"] + q))
                    for u, i, pp, s in items:
                        fb, hl, f4 = 4 * half + 2 * pp + i, 2 * (2 * pp + i) + s, 2 * pp + i
                        out = b_(n)[HD * s:HD * s + HD, f4 * HD:(f4 + 1) * HD]
                        mm(out, lhsT=r_bk[:, (2 * fb + s) * HD:][:, :HD], rhs=r_U[:, hl * HD:(hl + 1) * HD],
                           start=True, stop=False, tile_position=(0, HD * s))
                        ins = mm(out, lhsT=r_bk[:, D + (2 * fb + s) * HD:][:, :HD],
                                 rhs=r_vt[:, tile, (2 * fb + s) * HD:][:, :HD], start=False, stop=True,
                                 tile_position=(0, HD * s))
                    ins.then_inc(psum_full, 1)

            for d in range(2):
                rw_direction(d)
            pe.wait_ge(gate_sigmoid, 1)
            for c in range(2):
                for tt in range(TT):
                    n = G["gate"] + 2 * c + tt
                    if n >= BANKS:
                        pe.wait_ge(*when_read(n - BANKS))
                    mm(b_(n), lhsT=r_sg[:, tt * P:(tt + 1) * P], rhs=wl[:, 2 * D + c * 512:][:, :512],
                       start=True, stop=False)
                    mm(b_(n), lhsT=r_sg[0:32, T + tt * P:][:, :P], rhs=wl[0:32, 3 * D + c * 512:][:, :512],
                            start=False, stop=True).then_inc(psum_full, 1)
            for c in range(2):
                for tt in range(TT):
                    pe.wait_ge(*when_read(G["gate"] + 2 * c + tt))
            for q in range(4):
                transposes(G["tx_y"] + q, [r_yt[:, tt, (2 * q + f) * P:][:, :P] for f in range(2) for tt in range(TT)])
            for q in range(4):
                pe.wait_ge(*when_read(G["tx_y"] + q))
            square_tokens("rw_o", r_oT)
            ffn(2, 8)

        @block.vector
        def _(dve):
            steps = [0]

            def step(instruction):
                steps[0] += 1
                instruction.then_inc(dve_step, 1)

            def settle():
                dve.wait_ge(dve_step, steps[0])

            V = nc.vector
            tt_ = V.tensor_tensor
            ts_ = V.tensor_scalar
            stt = V.scalar_tensor_tensor

            def do(instruction):
                step(instruction)
                settle()

            def normalise(k, src, out):
                for tt in range(TT):
                    dve.wait_ge(rstd_ready, RSTD_AT[k] + tt)
                    ts_(out[:, tt, :], src[:, tt, :], rstd[:, 2 * k + tt:2 * k + tt + 1], None, ALU.mult).then_inc(normed, 1)

            def transposed(n, dst, gain):
                for tt in range(TT):
                    for q in range(2):
                        m = n + 2 * tt + q
                        dve.wait_ge(psum_full, m + 1)
                        tt_(dst[:, 4 * q:4 * q + 4, tt * P:(tt + 1) * P], b3(m, 4, P),
                                     spread(col(gain, 4 * q, 4), P), ALU.mult).then_inc(bank_sem(m), 1)

            def residual(name):
                for c in range(2):
                    for tt in range(TT):
                        n = G[name] + 2 * c + tt
                        dve.wait_ge(psum_full, n + 1)
                        part = x[:, tt, c * 512:(c + 1) * 512]
                        tt_(part, part, b_(n), ALU.add).then_inc(bank_sem(n), 1)

            do(V.memset(mhalf, -0.5))
            V.memset(hT_flat[:, :], 0.0).then_inc(constants_made, 1)
            normalise(0, x, xn)
            normalise(1, memraw, memraw)
            dve.wait_ge(in_prm, 16)
            halves = [col("conv_w", 0, 4 * CONVB), col("conv_b", 0, CONVB), col("fcw0", 0, 3 * FB), col("fcb0", 0, FB),
                      col("w0", 0, 16), col("a0", 0, 16)]
            for i in (1, 2):
                halves += [col(f"fcw{i}", t * 2 * FB, FB) for t in range(3)] + [col(f"fcb{i}", 0, FB)]
            dve.wait_ge(s5_dt, 1)
            for part in halves:
                step(ts_(part, part, 0.5, None, ALU.mult))
            step(ts_(ka_h, col("k_a", 0, 8), 0.5, None, ALU.mult))
            ts_(ka_1, col("k_a", 0, 8), -0.5, 1.0, ALU.mult, ALU.add).then_inc(halved, 1)
            do(ts_(s_lr, col("lam_re", 0, 8), -1e-4, None, ALU.min))
            li = col("lam_im", 0, 8)
            tt_(s_lrdt, s_lr, s_dt, ALU.mult).then_inc(s5_lrdt, 1)
            do(tt_(s_th, li, s_dt, ALU.mult))
            do(ts_(s_k, s_th, 1 / (2 * math.pi), 1.5 * 2 ** 23, ALU.mult, ALU.add))
            do(ts_(s_k, s_k, -1.5 * 2 ** 23, None, ALU.add))
            two_pi = 2 * math.pi
            hi = 6.28125
            do(stt(s_r, s_k, -hi, s_th, ALU.mult, ALU.add))
            do(stt(s_r, s_k, -(two_pi - hi), s_r, ALU.mult, ALU.add))
            do(ts_(s_r, s_r, 3.1415925, -3.1415925, ALU.min, ALU.max))
            do(stt(s_abs, s_r, -1.0, s_r, ALU.mult, ALU.min))
            ts_(s_abs, s_abs, math.pi / 2, None, ALU.add).then_inc(s5_angle, 1)
            dve.wait_ge(s5_mag, 1)
            dve.wait_ge(s5_trig, 1)
            step(ts_(s_nsin, s_sin, -1.0, None, ALU.mult))
            step(tt_(s_abi, s_mag, s_sin, ALU.mult))
            do(tt_(s_abr, s_mag, s_cos, ALU.mult))
            ts_(s_abr, s_abr, -1.0, None, ALU.add).then_inc(s5_unit, 1)
            dve.wait_ge(s5_unit, 1)
            step(tt_(s_den, s_lr, s_lr, ALU.mult))
            do(tt_(s_t1, li, li, ALU.mult))
            do(tt_(s_den, s_den, s_t1, ALU.add))
            step(V.reciprocal(s_den, s_den))
            step(tt_(s_fr, s_abr, s_lr, ALU.mult))
            step(tt_(s_t1, s_abi, li, ALU.mult))
            step(tt_(s_fi, s_abi, s_lr, ALU.mult))
            do(tt_(s_t2, s_abr, li, ALU.mult))
            step(tt_(s_fr, s_fr, s_t1, ALU.add))
            do(tt_(s_fi, s_fi, s_t2, ALU.subtract))
            step(tt_(s_fr, s_fr, s_den, ALU.mult))
            do(tt_(s_fi, s_fi, s_den, ALU.mult))
            transposed(G["tx_mix"], h_mid, "mix_norm")
            transposed(G["tx_mem"], memT, "mem_norm")
            dve.wait_ge(in_s5c, 16)
            c3 = lambda ap: ap.rearrange("p (j c) -> p j c", j=S5_TILES)
            cr, ci = c3(s5c[:, 0:256]), c3(s5c[:, 256:512])
            wr, wi, t0 = c3(cw[:, 0:256]), c3(cw[:, 256:512]), c3(s5t[:, 4096:4352])
            step(tt_(wr, cr, spread(s_fr, 32), ALU.mult))
            do(tt_(t0, ci, spread(s_fi, 32), ALU.mult))
            do(tt_(wr, wr, t0, ALU.subtract))
            step(tt_(wi, cr, spread(s_fi, 32), ALU.mult))
            do(tt_(t0, ci, spread(s_fr, 32), ALU.mult))
            stt(wi, wi, -1.0, t0, ALU.mult, ALU.subtract).then_inc(s5_cw, 1)

            def xc_silu(i):
                dve.wait_ge(xc_tanh, i + 1)
                part = xc[:, 2 * i:2 * i + 2, :]
                stt(part, thA[:, (i % 2) * 512:][:, :512].rearrange("p (k t) -> p k t", k=2), 1.0, part,
                         ALU.add, ALU.mult).then_inc(xc_ready, 1)

            for i in range(7):
                n = G["xbc"] + i
                dve.wait_ge(xc_tap, i + 1)
                for s in (1, 2, 3):
                    for j in range(2):
                        fb = 2 * i + j
                        ins = stt(xc[:, fb, s:T], b_(n)[:, j * T:(j + 1) * T - s], col("conv_w", (3 - s) * CONVB + fb),
                                  xc[:, fb, s:T], ALU.mult, ALU.add)
                        if s < 3 or j == 0:
                            step(ins)
                    if s < 3:
                        settle()
                ins.then_inc(bank_sem(n), 1)
                if i >= 1:
                    xc_silu(i - 1)
            xc_silu(6)
            dve.wait_ge(in_rows, 16)
            n = G["dt"]
            dve.wait_ge(psum_full, n + 1)
            tt_(dxb.rearrange("p (t h) -> p t h", t=TT), b3(n, TT, HEADS), tiled(row("dt_bias", HEADS), TT), ALU.add).then_inc(bank_sem(n), 1)
            dve.wait_ge(*when_read(n))
            step(ts_(dtm, dxb, 0.0, None, ALU.max))
            stt(dte, dxb, -1.0, dxb, ALU.mult, ALU.min).then_inc(dt_neg, 1)
            for i in range(4):
                n = G["z"] + i
                dve.wait_ge(z_tanh, i + 1)
                tt = i % 2
                cols, width = (slice(0, 256), 256) if i < 2 else (slice(256, 768), 512)
                ins = stt(zs[:, tt, cols], thA[:, (i % 2) * 512:][:, :width], 1.0, b_(n, width), ALU.add, ALU.mult)
                ins.then_inc(bank_sem(n), 1)
            dve.wait_ge(s5_table, 1)
            for j in range(S5_TILES):
                n = G["s5_bu"] + j
                dve.wait_ge(psum_full, n + 1)
                two = lambda ap: ap.rearrange("p (r t) -> p r t", r=2)
                step(tt_(two(sp1), b3(n, 2, T), tiled(Er[:, j, :], 2), ALU.mult))
                tt_(two(sp2), b3(n, 2, T), tiled(Ei[:, j, :], 2), ALU.mult).then_inc(bank_sem(n), 1)
                settle()
                dve.wait_ge(*when_read(n))
                step(tt_(sgin[:, 0:T], sp1[:, 0:T], sp2[:, T:2 * T], ALU.subtract))
                do(tt_(sgin[:, T:2 * T], sp2[:, 0:T], sp1[:, T:2 * T], ALU.add))
                if j >= 2:
                    dve.wait_ge(s5_h, j - 1)
                for r in range(2):
                    ins = V.tensor_tensor_scan(sgs[j % 2][:, r * T:(r + 1) * T], s_mag[:, j:j + 1].to_broadcast([P, T]),
                                               sgin[:, r * T:(r + 1) * T], 0.0, ALU.mult, ALU.add)
                ins.then_inc(s5_scanned, 1)
                if j == 1:
                    dve.wait_ge(dt_ln, 1)
                    do(tt_(dts, dts, dtm, ALU.add))
                    two_h = lambda ap: ap.rearrange("p (t h) -> p t h", t=TT)
                    stt(two_h(da), two_h(dts), -1.0, tiled(aneg, TT), ALU.mult, ALU.mult).then_inc(da_ready, 1)
            n = G["acs"]
            dve.wait_ge(psum_full, n + 1)
            V.tensor_copy(acs, b_(n, 48)).then_inc(bank_sem(n), 1)
            dve.wait_ge(*when_read(n))
            tt_(dec, acs[:, 24:48], acs[:, 0:24], ALU.subtract).then_inc(acs_sub, 1)
            for q in range(3):
                dve.wait_ge(*when_read(G["x_tok"] + q))
            h64 = lambda ap: ap.rearrange("p (h c) -> p h c", c=HD)
            for tt in range(TT):
                step(tt_(h64(xdt_t[:, tt, :]), h64(xtok[:, tt, :]), spread(dts[:, tt * HEADS:(tt + 1) * HEADS], HD), ALU.mult))
            for tt in range(TT):
                step(tt_(h64(y_t[:, tt, :]), h64(xtok[:, tt, :]), spread(row("ssd_d", HEADS), HD), ALU.mult))
            settle()
            dve.wait_ge(decays, 1)
            tt_(h64(xdtd), h64(xdt_t[:, 0, :]), spread(dec[:, 0:HEADS], HD), ALU.mult).then_inc(xdt_ready, 1)
            n = G["s5_y"]
            dve.wait_ge(psum_full, n + 1)
            for k in range(2):
                ins = stt(y5g[:, k * T:(k + 1) * T], uT3[:, k, :], col("s5_d", k), b_(n)[:, k * T:(k + 1) * T],
                          ALU.mult, ALU.add)
            ins.then_inc(bank_sem(n), 1)
            dve.wait_ge(*when_read(n))
            y5, y5t = y5g[:, 0:512], y5g[:, 512:1024]
            do(tt_(y5t, y5, y5, ALU.mult))
            do(ts_(y5t, y5t, 0.044715, 1.0, ALU.mult, ALU.add))
            tt_(y5t, y5t, y5, ALU.mult).then_inc(s5_gelu_in, 1)
            dve.wait_ge(s5_gelu_tanh, 1)
            do(stt(y5, y5t, 1.0, y5, ALU.add, ALU.mult))
            ts_(y5, y5, 0.5, None, ALU.mult).then_inc(s5_gelu, 1)
            dve.wait_ge(*when_read(G["s5_glu"]))
            do(stt(y5T, y5t, 1.0, y5, ALU.add, ALU.mult))
            ts_(y5T, y5T, 0.5, None, ALU.mult).then_inc(s5_done, 1)
            for tt in range(TT):
                def trid(g):
                    if g >= 2:
                        dve.wait_ge(psum_full, G[f"row{tt}"] + g - 2 + 1)
                    elif tt:
                        dve.wait_ge(psum_full, G["row0"] + g + 2 + 1)
                    tt_(triD[:, (g % 2) * 384:][:, :384].rearrange("p (h l) -> p h l", h=HPG), tiled(c_("tri", P), HPG),
                             spread(da[:, tt * HEADS + HPG * g:][:, :HPG], P), ALU.mult).then_inc(trid_ready, 1)

                def lmask(g):
                    n = G[f"row{tt}"] + g
                    dve.wait_ge(psum_full, n + 1)
                    for i in range(HPG):
                        h = tt * HEADS + HPG * g + i
                        ins = stt(Lc[:, g * 384 + i * P:][:, :P], b_(n)[:, i * P:(i + 1) * P], acs[:, h:h + 1],
                                  c_("maskneg", P), ALU.subtract, ALU.min)
                    ins.then_inc(bank_sem(n), 1)

                def lmul(g):
                    dve.wait_ge(lc_exp, GROUPS * tt + g + 1)
                    part = Lc[:, g * 384:(g + 1) * 384].rearrange("p (h l) -> p h l", h=HPG)
                    dve.wait_ge(*when_read(G["cb"] + tt))
                    tt_(part, part, tiled(cb[:, tt * 512 + g * P:][:, :P], HPG), ALU.mult).then_inc(lc_ready, 1)

                if tt:
                    dve.wait_ge(psum_full, G["diag0"] + 1 + 1)
                for g in range(GROUPS + 2):
                    if g < GROUPS:
                        trid(g)
                    if 1 <= g <= GROUPS:
                        lmask(g - 1)
                    if g >= 2:
                        lmul(g - 2)
                for q in range(2):
                    n = G[f"diag{tt}"] + q
                    dve.wait_ge(psum_full, n + 1)
                    part = y_t[:, tt, 384 * q:384 * (q + 1)]
                    tt_(part, part, b_(n, 384), ALU.add).then_inc(bank_sem(n), 1)
                if tt == 0:
                    for q in range(2):
                        dve.wait_ge(*when_read(G["diag0"] + q))
                    stt(y_t[:, 0, :], y_t[:, 0, :], 0.5, zs[:, 0, :], ALU.mult, ALU.mult).then_inc(y_gated, 1)
            for q in range(2):
                n = G["off"] + q
                dve.wait_ge(psum_full, n + 1)
                tt_(h64(sp1[:, 0:384]), b3(n, 6, HD), spread(eacs[:, HEADS + 6 * q:][:, :6], HD), ALU.mult).then_inc(bank_sem(n), 1)
                dve.wait_ge(*when_read(n))
                part = y_t[:, 1, 384 * q:384 * (q + 1)]
                dve.wait_ge(*when_read(G["diag1"] + q))
                do(tt_(part, part, sp1[:, 0:384], ALU.add))
            stt(y_t[:, 1, :], y_t[:, 1, :], 0.5, zs[:, 1, :], ALU.mult, ALU.mult).then_inc(y_gated, 1)
            for tt in range(TT):
                dve.wait_ge(ssd_rstd, tt + 1)
                dve.wait_ge(y_gated, tt + 1)
                ts_(y_t[:, tt, :], y_t[:, tt, :], srstd[:, tt:tt + 1], None, ALU.mult).then_inc(y_normed, 1)
            for q in range(3):
                n = G["tx_ssd"] + q
                dve.wait_ge(psum_full, n + 1)
                tt_(yT[:, 2 * q:2 * q + 2, :], b3(n, 2, T), spread(col("ssd_norm", 2 * q, 2), T), ALU.mult).then_inc(bank_sem(n), 1)
            residual("w_out")
            normalise(2, x, xn)
            transposed(G["tx_xa"], h_mid, "xa_norm")
            for h in range(XA_H):
                n = G[f"xa_s{h}"]
                dve.wait_ge(psum_full, n + 1)
                at = slice(2 * h, 2 * h + 2)
                do(V.tensor_reduce(mx[:, at], b3(n, 2, T), AX, ALU.max))
                ts_(nb[:, at], mx[:, at], -1 / 16, None, ALU.mult).then_inc(xa_max, 1)
            for h in range(XA_H):
                dve.wait_ge(*when_read(G[f"xa_s{h}"]))
                at = slice(2 * h, 2 * h + 2)
                do(V.reciprocal(den[:, at], den[:, at]))
                for tt in range(TT):
                    part = p_xa[:, h * 512 + tt * T:][:, :T]
                    ins = ts_(part, part, den[:, 2 * h + tt:2 * h + tt + 1], None, ALU.mult)
                ins.then_inc(xa_p, 1)
            residual("xa_o")

            def ffn(i, k):
                normalise(k, x, xn)
                transposed(G[f"tx_ffn{i}"], h_mid, f"ffn_norm{i}")
                nb_ = FB if i == 0 else 2 * FB
                shifts = [(1, 1), (2, 0)] if i == 0 else [(1, 0), (-1, 2)]

                def taps(n, acc, first_fb):
                    for m, (s, tap) in enumerate(shifts):
                        for j in range(2):
                            fb = first_fb + j
                            out = acc[:, j * T + s:(j + 1) * T] if s > 0 else acc[:, j * T:(j + 1) * T + s]
                            src = b_(n)[:, j * T:(j + 1) * T - s] if s > 0 else b_(n)[:, j * T - s:(j + 1) * T]
                            ins = stt(out, src, col(f"fcw{i}", tap * nb_ + fb), out, ALU.mult, ALU.add)
                            if m == 0 or j == 0:
                                step(ins)
                        if m == 0:
                            settle()
                    ins.then_inc(bank_sem(n), 1)

                def finish(c):
                    at = 11 * i + c
                    acc, th, val = (f[:, (c % 2) * 512:][:, :512] for f in (f_acc, f_th, f_val))
                    n = G[f"up{i}"] + 2 * c
                    dve.wait_ge(gate_tanh, at + 1)
                    do(stt(th, th, 1.0, acc, ALU.add, ALU.mult))
                    out = actT[:, 2 * c:2 * c + 2, :].rearrange("p k t -> p (k t)")
                    if i == 0:
                        dve.wait_ge(psum_full, n + 1 + 1)
                        ins = tt_(out, th, b_(n + 1), ALU.mult)
                        ins.then_inc(bank_sem(n + 1), 1)
                        dve.wait_ge(*when_read(n + 1))
                        V.tensor_copy(mx[:, 0:1], mhalf).then_inc(act_ready, 1)
                    else:
                        dve.wait_ge(*when_read(n + 1))
                        tt_(out, th, val, ALU.mult).then_inc(act_ready, 1)

                for c in range(11):
                    n = G[f"up{i}"] + 2 * c
                    dve.wait_ge(gate_tap, 11 * i + c + 1)
                    taps(n, f_acc[:, (c % 2) * 512:][:, :512], 2 * c)
                    if i:
                        dve.wait_ge(value_tap, 11 * (i - 1) + c + 1)
                        taps(n + 1, f_val[:, (c % 2) * 512:][:, :512], FB + 2 * c)
                    if c:
                        finish(c - 1)
                finish(10)
                residual(f"down{i}")

            ffn(0, 3)
            dve.wait_ge(in_fnw, 16)
            for tt in range(TT):
                dve.wait_ge(rstd_ready, RSTD_AT[4] + tt)
                stt(x[:, tt, :], x[:, tt, :], rstd[:, 8 + tt:9 + tt], fnw, ALU.mult, ALU.mult).then_inc(x_final_norm, 1)
            for tt in range(TT):
                dve.wait_ge(x_final_norm, tt + 1)
            normalise(5, x, xn)
            transposed(G["tx_swa"], h_mid, "tok_norm0")
            h64b = lambda ap: ap.rearrange("p (h c) -> p h c", c=HD)
            for tt in range(TT):
                dve.wait_ge(qk_square, tt + 1)
                V.tensor_reduce(qss[:, 20 * tt:20 * tt + 20], h64b(w_sq), AX, ALU.add).then_inc(qk_sums, 1)
            dve.wait_ge(in_swc, 16)
            for tt in range(TT):
                dve.wait_ge(qk_rstd, tt + 1)
                qk = h64b(qkv[:, tt, 0:1280])
                do(tt_(qk, qk, spread(qss[:, 20 * tt:20 * tt + 20], HD), ALU.mult))
                step(tt_(qk[:, 0:16], qk[:, 0:16], tiled(row("q_gain", HD), 16), ALU.mult))
                do(tt_(qk[:, 16:20], qk[:, 16:20], tiled(row("k_gain", HD), 4), ALU.mult))
                x1, x2 = qk[:, :, 0:HALF_ROT], qk[:, :, HALF_ROT:2 * HALF_ROT]
                cos_ = tiled(swc[:, SWC["cos"] + tt * HALF_ROT:][:, :HALF_ROT], 20)
                sin_ = tiled(swc[:, SWC["sin"] + tt * HALF_ROT:][:, :HALF_ROT], 20)
                t = [w_pT[:, m * 160:(m + 1) * 160].rearrange("p (h c) -> p h c", h=20) for m in range(4)]
                for m, (a, b) in enumerate(((x1, cos_), (x2, sin_), (x2, cos_), (x1, sin_))):
                    step(tt_(t[m], a, b, ALU.mult))
                settle()
                step(tt_(x1, t[0], t[1], ALU.subtract))
                tt_(x2, t[2], t[3], ALU.add).then_inc(roped, 1)

            def window_scores(q):
                for i in range(4):
                    h = 4 * q + i
                    n = G[f"sw_s{q}"] + i
                    if h >= 8:
                        dve.wait_ge(psum_full, G[f"sw_t{q - 2}"] + i + 1)
                    dve.wait_ge(psum_full, n + 1)
                    sc = w_p[:, (h % 8) * 512:][:, :512]
                    at = slice(2 * h, 2 * h + 2)
                    tt_(sc, b_(n), swc[:, 0:512], ALU.min).then_inc(bank_sem(n), 1)
                    dve.wait_ge(*when_read(n))
                    do(V.tensor_reduce(mx[:, at], sc.rearrange("p (t k) -> p t k", t=TT), AX, ALU.max))
                    do(ts_(mx[:, at], mx[:, at], 1 / 8, row("sinks", 1, h), ALU.mult, ALU.max))
                    ts_(nb[:, at], mx[:, at], -1.0, None, ALU.mult).then_inc(sw_max, 1)

            def window_p(q):
                for i in range(4):
                    h = 4 * q + i
                    at = slice(2 * h, 2 * h + 2)
                    dve.wait_ge(sw_exp, h + 1)
                    do(tt_(den[:, at], den[:, at], dsk[:, at], ALU.add))
                    do(V.reciprocal(den[:, at], den[:, at]))
                    for tt in range(TT):
                        part = w_p[:, (h % 8) * 512 + tt * T:][:, :T]
                        ins = ts_(part, part, den[:, 2 * h + tt:2 * h + tt + 1], None, ALU.mult)
                    ins.then_inc(sw_p, 1)

            window_scores(0)
            for q in range(4):
                if q < 3:
                    window_scores(q + 1)
                window_p(q)
            residual("swa_o")
            ffn(1, 6)
            normalise(7, x, xn)
            do(V.memset(hT[:, :, 0:1], 0.0))
            do(V.memset(hT[:, :, T + 1:T + 2], 0.0))
            transposed(G["tx_rw"], h_mid, "tok_norm1")
            for i in range(4):
                dve.wait_ge(*when_read(G["tx_rw"] + i))
            do(tt_(x_diff, hT[:, :, 0:T], hT[:, :, 2:T + 2], ALU.add))
            do(stt(x_diff, x_diff, 0.5, h_mid, ALU.mult, ALU.subtract))

            def mix(k, buf):
                for kb in range(KB):
                    ins = stt(x_mix[buf][:, kb, :], x_diff[:, kb, :], col("mu", 8 * k + kb), h_mid[:, kb, :],
                              ALU.mult, ALU.add)
                ins.then_inc(x_mixed, 1)

            mix(0, 0)
            mix(2, 1)
            dve.wait_ge(psum_full, G["rw_r"] + 3 + 1)
            mix(3, 0)
            for i in range(4):
                n = G["rw_k"] + i
                dve.wait_ge(rw_k_copied, i + 1)
                for j in range(2):
                    ins = ts_(r_kk3[:, 2 * i + j, :], b_(n)[:, j * T:(j + 1) * T], col("k_k", 2 * i + j), None, ALU.mult)
                ins.then_inc(bank_sem(n), 1)
            mix(1, 1)
            dve.wait_ge(psum_full, G["rw_v"] + 3 + 1)
            mix(4, 0)
            n = G["kk_ss"]
            dve.wait_ge(psum_full, n + 1)
            ts_(r_X[0:16, 0:T], b_(n)[0:16, 0:T], 1e-24, None, ALU.max).then_inc(bank_sem(n), 1)
            dve.wait_ge(psum_full, G["lora1"] + 1)
            mix(5, 1)
            dve.wait_ge(*when_read(G["lora1"] + 1))
            step(ts_(r_sg[:, 0:T], r_sg[:, 0:T], 0.5, 0.5, ALU.mult, ALU.add))
            ts_(r_sg[0:32, T:2 * T], r_sg[0:32, T:2 * T], 0.5, 0.5, ALU.mult, ALU.add).then_inc(gate_sigmoid, 1)
            for q in range(4):
                n = G["kk_bc"] + q
                dve.wait_ge(psum_full, n + 1)
                part = r_kk3[:, 2 * q:2 * q + 2, :]
                tt_(part, part, b3(n, 2, T), ALU.mult).then_inc(bank_sem(n), 1)
            xn3 = three(xn_flat[:, :])
            hf3 = three(hflat)
            LA3 = three(r_LA)

            def sums_of_decays(d):
                for i in range(4):
                    dve.wait_ge(*when_read(G[f"wl{d}_{i}"]))
                do(ts_(hflat, hflat, 1.0, None, ALU.add))
                for fb in range(KB):
                    keep, src, out = c_(f"keep{d}", T), hf3[:, fb, :], xn3[:, fb, :]
                    if d:
                        keep, src, out = keep[:, ::-1], src[:, ::-1], out[:, ::-1]
                    step(V.tensor_tensor_scan(out, keep, src, 0.0, ALU.mult, ALU.add))
                settle()
                mid = r_mid.rearrange("p (k i) -> p k i", k=KB)
                tiles = xn_flat[:, :].rearrange("p (k i t) -> p k i t", k=KB, i=TT)
                do(V.tensor_copy(mid, tiles[:, :, :, 63]))
                fin = r_fin[:, 8 * d:8 * d + 8]
                do(tt_(fin, tiles[:, :, d, 0 if d else P - 1], mid[:, :, d], ALU.subtract))
                do(tt_(fin, fin, mid[:, :, 1 - d], ALU.add))
                flat = xn_flat[:, :].rearrange("p (k t) -> p k t", t=P)
                do(tt_(flat, flat, spread(r_mid, P), ALU.subtract))
                tt_(hflat, xn_flat[:, :], hflat, ALU.subtract).then_inc(cum_done, 1)

            def rw_prepare(d):
                if d == 0:
                    sums_of_decays(0)
                for i in range(4):
                    dve.wait_ge(*when_read(G[f"al{d}"] + i))
                for fb in range(KB):
                    step(ts_(r_kh3[:, fb, :], LA3[:, fb, :], ka_h[:, fb:fb + 1], ka_1[:, fb:fb + 1], ALU.mult, ALU.add))
                settle()
                do(ts_(r_LA, r_LA, 0.5, 0.5, ALU.mult, ALU.add))
                step(tt_(r_bh, r_LA, r_kk, ALU.mult))
                do(tt_(r_kh, r_kh, r_kT, ALU.mult))
                for fb in range(KB):
                    ins = stt(LA3[:, fb, :], r_kh3[:, fb, :], col("r_k", fb), r_rT3[:, fb, :], ALU.mult, ALU.mult)
                ins.then_inc(rks_ready, 1)
                dve.wait_ge(rks_ready, d + 1)
                dve.wait_ge(e_up, d + 1)
                step(tt_(r_kh, r_kh, r_TT, ALU.mult))
                both = r_AR.rearrange("p (k a t) -> p k a t", a=2, t=P)
                tiled_ = lambda ap: ap.rearrange("p (k t) -> p k t", t=P)
                dve.wait_ge(e_down, d + 1)
                step(tt_(both[:, :, 1, :], tiled_(r_rT), tiled_(xn_flat[:, :]), ALU.mult))
                dve.wait_ge(e_before, d + 1)
                stt(both[:, :, 0, :], tiled_(r_kk), -1.0, tiled_(hflat), ALU.mult, ALU.mult).then_inc(abkr_ready, 1)
                n = G[f"bonus{d}"]
                dve.wait_ge(psum_full, n + 1)
                if d == 0:
                    V.tensor_copy(r_bon, b_(n, 32)).then_inc(bank_sem(n), 1)
                else:
                    tt_(r_bon, r_bon, b_(n, 32), ALU.add).then_inc(bank_sem(n), 1)

            def products(b, j):
                d, half = int(b[0]), int(b[2])
                if j == 0:
                    if half:
                        dve.wait_ge(la_zero, d + 1)
                    else:
                        dve.wait_ge(l_zero, d + 1)
                n = G[f"ab{b}_{j}"]
                dve.wait_ge(psum_full, n + 1)
                dst = (LAs, LBs)[j // 4][half][:, j % 4 * 512:][:, :512]
                V.copy_predicated(dst.rearrange("p (i c) -> p i c", i=2),
                                           tiled(masks[:, MSK_DIR * d:MSK_DIR * d + 256], 2), b3(n, 2, 256)).then_inc(bank_sem(n), 1)

            def start_levels(d, order, half):
                for j in range(4):
                    dve.wait_ge(*when_read(G[f"ab{d}{order}{half}_{j}"]))
                at = BATCH_AT[d, order, half]
                dve.wait_ge(t_identity, at + 1)
                first = masks[:, MSK_DIR * d + 256 + P:][:, :P]
                V.copy_predicated(r_Tk[:, :, 1], tiled(first, 8), per_head(LAs[half])[:, :, 0]).then_inc(t_start, 1)

            def rw_batch(d, order, half, following):
                b = f"{d}{order}{half}"
                tile = order if d == 0 else 1 - order
                m0 = MSK_DIR * d
                for lv in range(1, LEVELS):
                    o = int(lv == LEVELS - 1)
                    mask = masks[:, m0 + 256 + 256 * lv + P * o:][:, :P]
                    for g2 in range(2):
                        n = level_groups(lv, b, g2)[2]
                        dve.wait_ge(psum_full, n + 1)
                        V.copy_predicated(r_Tk[:, 4 * g2:4 * g2 + 4, o], tiled(mask, 4), b3(n, 4, P)).then_inc(bank_sem(n), 1)
                    if following and lv <= 4:
                        products(following, 2 * lv - 2)
                        products(following, 2 * lv - 1)
                if following:
                    start_levels(*map(int, following))
                elif d == 0:
                    sums_of_decays(1)
                n = G["ys" + b]
                dve.wait_ge(psum_full, n + 1)
                part = r_yt[:, tile, half * 512:(half + 1) * 512]
                if d == 0:
                    V.tensor_copy(part, b_(n)).then_inc(bank_sem(n), 1)
                else:
                    tt_(part, part, b_(n), ALU.add).then_inc(bank_sem(n), 1)
                if order == 0:
                    n = G["ss" + b]
                    dve.wait_ge(psum_full, n + 1)
                    dve.wait_ge(e_state, d + 1)
                    for s in range(2):
                        at = slice(HD * s, HD * s + HD)
                        ins = tt_(r_S4[at, 4 * half:4 * half + 4, s, :], b3(n, 4, HD)[at],
                                  spread(r_fac[at, 8 * d + 4 * half:8 * d + 4 * half + 4], HD), ALU.mult)
                    ins.then_inc(bank_sem(n), 1)

            do(V.memset(r_S, 0.0))
            for d in range(2):
                rw_prepare(d)
                dve.wait_ge(abkr_ready, d + 1)
                settle()
                step(V.memset(LBs[0], 0.0))
                settle()
                for j in range(8):
                    products(BATCHES[d][0], j)
                start_levels(d, 0, 0)
                for at in range(4):
                    rw_batch(d, at // 2, at % 2, BATCHES[d][at + 1] if at < 3 else None)
            for half in (0, 1):
                for order in (0, 1):
                    dve.wait_ge(*when_read(G[f"ys1{order}{half}"]))
            y32 = r_y.rearrange("p (h c) -> p h c", c=HD)
            do(V.tensor_reduce(gn_s, y32, AX, ALU.add))
            do(ts_(gn_m, gn_s, 1 / HD, None, ALU.mult))
            tt_(y32, y32, spread(gn_m, HD), ALU.subtract).then_inc(y_centred, 1)
            v32 = r_v.rearrange("p (h c) -> p h c", c=HD)
            dve.wait_ge(*when_read(G["bonus1"]))
            do(tt_(v32, v32, spread(r_bon, HD), ALU.mult))
            dve.wait_ge(gn_square, 1)
            V.tensor_reduce(gn_q, r_AR[:, 0:2048].rearrange("p (h c) -> p h c", c=HD), AX, ALU.add).then_inc(gn_sums, 1)
            dve.wait_ge(gn_rstd, 1)
            dve.wait_ge(y_centred, 1)
            do(tt_(y32, y32, spread(gn_q, HD), ALU.mult))
            dve.wait_ge(in_lnx, 32)
            do(tt_(r_yt, r_yt, tiled(lnx[:, 0:D], TT), ALU.mult))
            do(tt_(r_yt, r_yt, tiled(lnx[:, D:2 * D], TT), ALU.add))
            do(tt_(r_y, r_y, r_v, ALU.add))
            for c in range(2):
                for tt in range(TT):
                    n = G["gate"] + 2 * c + tt
                    dve.wait_ge(psum_full, n + 1)
                    part = r_yt[:, tt, c * 512:(c + 1) * 512]
                    tt_(part, part, b_(n), ALU.mult).then_inc(bank_sem(n), 1)
            residual("rw_o")
            ffn(2, 8)

        @block.gpsimd
        def _(pool):
            steps = [0]

            def step(instruction):
                steps[0] += 1
                instruction.then_inc(pool_step, 1)

            def settle():
                pool.wait_ge(pool_step, steps[0])

            g = nc.gpsimd

            def do(instruction):
                step(instruction)
                settle()

            def inverse_root(out, src, n, count, eps, name):
                do(g.tensor_scalar(src, src, 1 / count, eps, ALU.mult, ALU.add))
                g.tensor_tensor(out, src, mhalf[0:src.shape[0]].to_broadcast([src.shape[0], n]), ALU.pow).then_inc(name, 1)

            def rms(k):
                for tt in range(TT):
                    pool.wait_ge(sumsq, SUMSQ_AT[k] + tt)
                    at = slice(2 * k + tt, 2 * k + tt + 1)
                    inverse_root(rstd[:, at], ss[:, at], 1, D, EPS, rstd_ready)

            pool.wait_ge(constants_made, 1)
            rms(0)
            rms(1)
            m = g.tensor_tensor
            pool.wait_ge(s5_unit, 1)
            step(g.memset(Er[:, :, 0:1], 1.0))
            step(g.memset(Ei[:, :, 0:1], 0.0))
            one = lambda ap: ap.unsqueeze(2)
            step(g.tensor_copy(Er[:, :, 1:2], one(s_cos)))
            step(g.tensor_copy(Ei[:, :, 1:2], one(s_nsin)))
            step(g.tensor_copy(s_pr, s_cos))
            do(g.tensor_copy(s_pi, s_nsin))
            k = 1
            while 2 * k < T:
                step(m(s_qr, s_pr, s_pr, ALU.mult))
                step(m(s_qi, s_pi, s_pi, ALU.mult))
                do(m(s_pi, s_pr, s_pi, ALU.mult))
                step(m(s_pr, s_qr, s_qi, ALU.subtract))
                do(g.tensor_scalar(s_pi, s_pi, 2.0, None, ALU.mult))
                k *= 2
                cols, nxt = slice(0, k), slice(k, 2 * k)
                a = s5t[:, 3072:3072 + 8 * k].rearrange("p (j t) -> p j t", j=S5_TILES)
                b = cb[:, 0:8 * k].rearrange("p (j t) -> p j t", j=S5_TILES)
                pr, pi = spread(s_pr, k), spread(s_pi, k)
                step(m(a, Er[:, :, cols], pr, ALU.mult))
                do(m(b, Ei[:, :, cols], pi, ALU.mult))
                do(m(Er[:, :, nxt], a, b, ALU.subtract))
                step(m(a, Er[:, :, cols], pi, ALU.mult))
                do(m(b, Ei[:, :, cols], pr, ALU.mult))
                last = m(Ei[:, :, nxt], a, b, ALU.add)
                if 2 * k < T:
                    do(last)
                else:
                    last.then_inc(s5_table, 1)
            two = lambda ap: ap.rearrange("p (r t) -> p r t", r=2)
            for j in range(S5_TILES):
                pool.wait_ge(s5_scanned, j + 1)
                src = sgs[j % 2]
                if j:
                    pool.wait_ge(s5_h, j)
                step(m(two(sq1), two(src), tiled(Er[:, j, :], 2), ALU.mult))
                do(m(two(sq2), two(src), tiled(Ei[:, j, :], 2), ALU.mult))
                settle()
                step(m(Er[:, j, :], sq1[:, 0:T], sq2[:, T:2 * T], ALU.add))
                m(Ei[:, j, :], sq1[:, T:2 * T], sq2[:, 0:T], ALU.subtract).then_inc(s5_h, 1)
            for tt in range(TT):
                pool.wait_ge(ssd_sumsq, tt + 1)
                inverse_root(srstd[:, tt:tt + 1], ssn[:, tt:tt + 1], 1, INNER, EPS, ssd_rstd)
            rms(2)
            rms(3)
            rms(4)
            rms(5)
            for tt in range(TT):
                pool.wait_ge(qk_sums, tt + 1)
                part = qss[:, 20 * tt:20 * tt + 20]
                inverse_root(part, part, 20, HD, EPS, qk_rstd)
            rms(6)
            rms(7)
            pool.wait_ge(in_masks, 16)
            g.tensor_copy(masks[:, :], masks_in).then_inc(masks_made, 1)
            pool.wait_ge(*when_read(G["kk_ss"]))
            part = r_X[0:16, 0:T]
            m(part, part, mhalf[0:16].to_broadcast([16, T]), ALU.pow).then_inc(kk_rnorm, 1)
            for d in range(2):
                pool.wait_ge(rks_ready, d + 1)
                pool.wait_ge(e_up, d + 1)
                m(r_bh, r_bh, r_TT, ALU.mult).then_inc(b_scaled, 1)
                pool.wait_ge(psum_full, G[f"bonus{d}"] + 1)
                step(g.memset(r_LB, 0.0))
                g.memset(r_LA, 0.0).then_inc(la_zero, 1)
                pool.wait_ge(abkr_ready, d + 1)
                g.memset(LAs[0], 0.0).then_inc(l_zero, 1)
                pool.wait_ge(b_scaled, d + 1)
                for order in (0, 1):
                    for half in (0, 1):
                        at = BATCH_AT[d, order, half]
                        if at % 4:
                            pool.wait_ge(psum_full, G[f"us{d}{(at - 1) // 2 % 2}{(at - 1) % 2}"] + 1)
                        g.tensor_copy(r_Tk[:, :, 1], tiled(ident, 8)).then_inc(t_identity, 1)
            pool.wait_ge(gn_sums, 1)
            inverse_root(gn_q, gn_q, 32, HD, GN_EPS, gn_rstd)
            rms(8)


def kernel(**inputs):
    import concourse.bacc as bacc
    from concourse.bass_utils import run_bass_kernel_spmd

    arrays = lay_out({k: np.asarray(v) for k, v in inputs.items()})
    nc = bacc.Bacc("TRN2", target_bir_lowering=False, num_devices=1)
    io = {}
    for name, a in arrays.items():
        io[name] = nc.dram_tensor(f"in_{name}", a.shape, mybir.dt.from_np(a.dtype), kind="ExternalInput").ap()
    io["y"] = nc.dram_tensor("out_y", (T, D), F32, kind="ExternalOutput").ap()
    build(nc, io)
    r = run_bass_kernel_spmd(nc, [{f"in_{k}": v for k, v in arrays.items()}], core_ids=[0])
    return r.results[0]["out_y"].reshape(1, T, D)
```
